# Optimizing a Trainium2 kernel written in Bass

```python
import jax, jax.numpy as jnp
from jax import lax
import numpy as np

D_MODEL = 1024
BATCH = 1
SEQ = 512
DEPTH = 2
DEC_BATCH = 1
DEC_SEQ = 32
PAST_LEN = 256

CHUNK = 64
QBLK = 128
RBLK = 16
N_AB = (DEPTH + 1) // 2
N_CD = DEPTH // 2

A_HEADS = 4
A_DK = 128
A_DV = 128
B_HEADS = 4
B_DK = 64
B_DV = 128
B_GATE_RANK = 16
B_GATE_NORM = 16.0
C_HEADS = 8
C_HD = 64
D_HEADS = 8
D_KV_HEADS = 2
D_HD = 64
IDX_HEADS = 4
IDX_DIM = 64
IDX_TOPK_MAX = 256
IDX_SCALE = (IDX_DIM ** -0.5) * (IDX_HEADS ** -0.5)
FFN_HIDDEN = ((8 * D_MODEL // 3 + 255) // 256) * 256

AB_SIZES = (A_HEADS * A_DK, A_HEADS * A_DK, A_HEADS * A_DV, A_HEADS * A_DV,
            B_HEADS * B_DK, B_HEADS * B_DK, B_HEADS * B_DV, B_HEADS * B_DV, B_GATE_RANK)
AB_IN = sum(AB_SIZES)
AB_MIX = A_HEADS * A_DV + B_HEADS * B_DV
CD_SIZES = (C_HEADS * C_HD, C_HEADS * C_HD, C_HEADS * C_HD, C_HEADS,
            D_HEADS * D_HD, D_KV_HEADS * D_HD, D_KV_HEADS * D_HD, IDX_HEADS * IDX_DIM, IDX_DIM, IDX_HEADS)
CD_IN = sum(CD_SIZES)
CD_MIX = C_HEADS * C_HD + D_HEADS * D_HD
F32 = jnp.float32

kernel_name = "hybrid_stream_hgrn2_gla_fox_dsa"

def rmsnorm(x, g, eps=1e-6):
    xf = x.astype(F32)
    y = xf * lax.rsqrt(jnp.mean(xf * xf, axis=-1, keepdims=True) + eps) * g.astype(F32)
    return y.astype(x.dtype)

def split_cols(h, sizes):
    return jnp.split(h, [int(o) for o in np.cumsum(sizes)[:-1]], axis=-1)

def heads(z, n):
    return z.reshape(z.shape[:-1] + (n, z.shape[-1] // n))

def to_blocks(z, nb, blk):
    return z.reshape((z.shape[0], nb, blk) + z.shape[2:]).swapaxes(0, 1)

def from_blocks(z):
    return z.swapaxes(0, 1).reshape((z.shape[1], z.shape[0] * z.shape[2]) + z.shape[3:])

def gated_linear_recurrence(q, k, v, log_a, s0):
    t_len = q.shape[1]
    n_blk = -(-t_len // RBLK)
    pad = ((0, 0), (0, n_blk * RBLK - t_len), (0, 0), (0, 0))
    qb, kb, vb, ab = (to_blocks(jnp.pad(z.astype(F32), pad), n_blk, RBLK) for z in (q, k, v, log_a))
    causal = jnp.tril(jnp.ones((RBLK, RBLK), dtype=bool))

    def step(s, blk):
        qc, kc, vc, ac = blk
        b = jnp.cumsum(ac, axis=1)
        b_last = b[:, -1]
        q_dec = qc * jnp.exp(b)
        att = jnp.einsum('blhk,bmhk->bhlm', q_dec, kc * jnp.exp(-b))
        att = jnp.where(causal, att, 0.0)
        o = jnp.einsum('blhk,bhkv->blhv', q_dec, s) + jnp.einsum('bhlm,bmhv->blhv', att, vc)
        s_new = jnp.exp(b_last)[..., None] * s + jnp.einsum(
            'blhk,blhv->bhkv', kc * jnp.exp(b_last[:, None] - b), vc)
        return s_new, o

    s_final, o = lax.scan(step, s0.astype(F32), (qb, kb, vb, ab))
    return from_blocks(o)[:, :t_len], s_final

def ab_mixer(xn, w_in, w_out, lower_bound, a_gnorm, w_gk, b_gk, b_gnorm, s_a, s_b):
    bsz, t_len = xn.shape[:2]
    h = jnp.einsum('btd,de->bte', xn, w_in)
    a_q, a_f, a_i, a_g, b_q, b_k, b_v, b_g, b_lr = split_cols(h, AB_SIZES)
    f = lower_bound + (1.0 - lower_bound) * jax.nn.sigmoid(a_f.astype(F32))
    o_a, s_a_new = gated_linear_recurrence(
        heads(jax.nn.silu(a_q), A_HEADS), heads(1.0 - f, A_HEADS), heads(a_i, A_HEADS),
        heads(jnp.log(f), A_HEADS), s_a)
    o_a = rmsnorm(o_a, a_gnorm) * jax.nn.silu(heads(a_g, A_HEADS).astype(F32))
    gk = jnp.einsum('btr,rk->btk', b_lr, w_gk) + b_gk
    log_alpha = jax.nn.log_sigmoid(gk.astype(F32)) / B_GATE_NORM
    o_b, s_b_new = gated_linear_recurrence(
        heads(b_q * (B_DK ** -0.5), B_HEADS), heads(b_k, B_HEADS), heads(b_v, B_HEADS),
        heads(log_alpha, B_HEADS), s_b)
    o_b = rmsnorm(o_b, b_gnorm) * jax.nn.silu(heads(b_g, B_HEADS).astype(F32))
    o = jnp.concatenate([o_a.reshape(bsz, t_len, -1), o_b.reshape(bsz, t_len, -1)], axis=-1).astype(xn.dtype)
    return jnp.einsum('bte,ed->btd', o, w_out), s_a_new, s_b_new

def fox_attention(q, k_all, v_all, logf_all, q_start):
    bsz, tq, h, hd = q.shape
    s_len = k_all.shape[1]
    qblk = min(QBLK, tq)
    nb = tq // qblk
    cum = jnp.cumsum(logf_all.astype(F32), axis=1)
    cum_q = lax.slice_in_dim(cum, q_start, q_start + tq, axis=1)
    cum_t = cum.transpose(0, 2, 1)
    key_pos = jnp.arange(s_len)
    q_pos = q_start + jnp.arange(tq)

    def block(args):
        qb, cqb, pb = args
        logits = jnp.einsum('bqhd,bshd->bhqs', qb, k_all).astype(F32) * (hd ** -0.5)
        logits = logits + cqb.transpose(0, 2, 1)[..., None] - cum_t[:, :, None, :]
        logits = jnp.where(key_pos[None, None, None, :] <= pb[None, None, :, None], logits, -jnp.inf)
        p = jax.nn.softmax(logits, axis=-1)
        return jnp.einsum('bhqs,bshd->bqhd', p.astype(v_all.dtype), v_all)

    out = lax.map(block, (to_blocks(q, nb, qblk), to_blocks(cum_q, nb, qblk), q_pos.reshape(nb, qblk)))
    return from_blocks(out)

def dsa_attention(q, k_all, v_all, iq, iw, ik_all, q_start):
    bsz, tq, h, hd = q.shape
    s_len, g = k_all.shape[1], k_all.shape[2]
    topk = min(IDX_TOPK_MAX, s_len // 4)
    qblk = min(QBLK, tq)
    nb = tq // qblk
    key_chunk = jnp.arange(s_len) // CHUNK
    q_pos = q_start + jnp.arange(tq)
    gather_rows = jax.vmap(lambda rows, idx: rows[idx])

    def block(args):
        qb, iqb, iwb, pb = args
        q_chunk = pb // CHUNK
        score = jax.nn.relu(jnp.einsum('bqhd,bsd->bqhs', iqb, ik_all).astype(F32))
        score = jnp.einsum('bqhs,bqh->bqs', score, iwb.astype(F32)) * IDX_SCALE
        admissible = key_chunk[None, :] <= q_chunk[:, None]
        score = jnp.where(admissible[None], score, -jnp.inf)
        _, idx = lax.top_k(score, topk)
        valid = key_chunk[idx] <= q_chunk[None, :, None]
        k_sel = gather_rows(k_all, idx)
        v_sel = gather_rows(v_all, idx)
        qg = qb.reshape(bsz, qblk, g, h // g, hd)
        logits = jnp.einsum('bqgnd,bqkgd->bqgnk', qg, k_sel).astype(F32) * (hd ** -0.5)
        logits = jnp.where(valid[:, :, None, None, :], logits, -jnp.inf)
        p = jax.nn.softmax(logits, axis=-1)
        o = jnp.einsum('bqgnk,bqkgd->bqgnd', p.astype(v_sel.dtype), v_sel)
        return o.reshape(bsz, qblk, h, hd)

    out = lax.map(block, (to_blocks(q, nb, qblk), to_blocks(iq, nb, qblk), to_blocks(iw, nb, qblk),
                          q_pos.reshape(nb, qblk)))
    return from_blocks(out)

def cd_mixer(xn, w_in, f_bias, w_out, cache):
    bsz, t_len = xn.shape[:2]
    h = jnp.einsum('btd,de->bte', xn, w_in)
    c_q, c_k, c_v, c_f, d_q, d_k, d_v, d_iq, d_ik, d_iw = split_cols(h, CD_SIZES)
    c_q, c_k, c_v = heads(c_q, C_HEADS), heads(c_k, C_HEADS), heads(c_v, C_HEADS)
    c_logf = jax.nn.log_sigmoid(c_f.astype(F32) + f_bias.astype(F32))
    d_q, d_k, d_v = heads(d_q, D_HEADS), heads(d_k, D_KV_HEADS), heads(d_v, D_KV_HEADS)
    d_iq = heads(d_iq, IDX_HEADS)
    rows = (c_k, c_v, c_logf, d_k, d_v, d_ik)
    if cache is None:
        q_start, keys = 0, rows
    else:
        q_start = cache[0].shape[1]
        keys = [jnp.concatenate([c.astype(r.dtype), r], axis=1) for c, r in zip(cache, rows)]
    fk, fv, flogf, dk, dv, dik = keys
    o_c = fox_attention(c_q, fk, fv, flogf, q_start)
    o_d = dsa_attention(d_q, dk, dv, d_iq, d_iw, dik, q_start)
    o = jnp.concatenate([o_c.reshape(bsz, t_len, -1), o_d.reshape(bsz, t_len, -1)], axis=-1).astype(xn.dtype)
    return jnp.einsum('bte,ed->btd', o, w_out), rows

def swiglu(xn, w_in, w_out):
    gate, up = jnp.split(jnp.einsum('btd,df->btf', xn, w_in), 2, axis=-1)
    return jnp.einsum('btf,fd->btd', jax.nn.silu(gate) * up, w_out)

def run_trunk(x, hgrn_s, gla_s, cd_cache, norm_mix, norm_ffn, norm_final, ab_w_in, ab_w_out,
              hgrn_lb_logits, hgrn_gnorm, gla_w_gk, gla_b_gk, gla_gnorm, cd_w_in, cd_w_out,
              fox_f_bias, ffn_w_in, ffn_w_out):
    lbs = jnp.cumsum(jax.nn.softmax(hgrn_lb_logits.astype(F32), axis=0), axis=0)
    new_hgrn, new_gla, new_cd = [], [], []
    for layer in range(DEPTH):
        li = layer // 2
        xn = rmsnorm(x, norm_mix[layer])
        if layer % 2 == 0:
            y, sa, sb = ab_mixer(xn, ab_w_in[li], ab_w_out[li], lbs[li], hgrn_gnorm[li], gla_w_gk[li],
                                 gla_b_gk[li], gla_gnorm[li], hgrn_s[li], gla_s[li])
            new_hgrn.append(sa)
            new_gla.append(sb)
        else:
            cache = None if cd_cache is None else [c[li] for c in cd_cache]
            y, rows = cd_mixer(xn, cd_w_in[li], fox_f_bias[li], cd_w_out[li], cache)
            new_cd.append(rows)
        x = x + y
        x = x + swiglu(rmsnorm(x, norm_ffn[layer]), ffn_w_in[layer], ffn_w_out[layer])
    cd_rows = [jnp.stack([r[j] for r in new_cd]) for j in range(6)]
    return (rmsnorm(x, norm_final), jnp.stack(new_hgrn), jnp.stack(new_gla), *cd_rows)

def setup_inputs(seed: int = 0) -> dict:
    key = jax.random.key(seed)
    ks = iter(jax.random.split(key, 32))

    def nrm(shape, scale=1.0, offset=0.0):
        return offset + scale * jax.random.normal(next(ks), shape, dtype=F32)

    return {
        'x_prompt': nrm((BATCH, SEQ, D_MODEL)),
        'x_sample': nrm((DEC_BATCH, DEC_SEQ, D_MODEL)),
        'state_hgrn': nrm((N_AB, DEC_BATCH, A_HEADS, A_DK, A_DV), 0.5),
        'state_gla': nrm((N_AB, DEC_BATCH, B_HEADS, B_DK, B_DV), 1.0),
        'cache_fox_k': nrm((N_CD, DEC_BATCH, PAST_LEN, C_HEADS, C_HD)),
        'cache_fox_v': nrm((N_CD, DEC_BATCH, PAST_LEN, C_HEADS, C_HD)),
        'cache_fox_logf': jax.nn.log_sigmoid(nrm((N_CD, DEC_BATCH, PAST_LEN, C_HEADS), 0.5, 2.0)),
        'cache_dsa_k': nrm((N_CD, DEC_BATCH, PAST_LEN, D_KV_HEADS, D_HD)),
        'cache_dsa_v': nrm((N_CD, DEC_BATCH, PAST_LEN, D_KV_HEADS, D_HD)),
        'cache_dsa_ik': nrm((N_CD, DEC_BATCH, PAST_LEN, IDX_DIM)),
        'norm_mix': nrm((DEPTH, D_MODEL), 0.05, 1.0),
        'norm_ffn': nrm((DEPTH, D_MODEL), 0.05, 1.0),
        'norm_final': nrm((D_MODEL,), 0.05, 1.0),
        'ab_w_in': nrm((N_AB, D_MODEL, AB_IN), D_MODEL ** -0.5),
        'ab_w_out': nrm((N_AB, AB_MIX, D_MODEL), AB_MIX ** -0.5),
        'hgrn_lb_logits': nrm((N_AB + 1, A_HEADS * A_DK), 0.5),
        'hgrn_gnorm': nrm((N_AB, A_DV), 0.05, 1.0),
        'gla_w_gk': nrm((N_AB, B_GATE_RANK, B_HEADS * B_DK), B_GATE_RANK ** -0.5),
        'gla_b_gk': nrm((N_AB, B_HEADS * B_DK), 0.1),
        'gla_gnorm': nrm((N_AB, B_DV), 0.05, 1.0),
        'cd_w_in': nrm((N_CD, D_MODEL, CD_IN), D_MODEL ** -0.5),
        'cd_w_out': nrm((N_CD, CD_MIX, D_MODEL), CD_MIX ** -0.5),
        'fox_f_bias': nrm((N_CD, C_HEADS), 0.1, 2.0),
        'ffn_w_in': nrm((DEPTH, D_MODEL, 2 * FFN_HIDDEN), D_MODEL ** -0.5),
        'ffn_w_out': nrm((DEPTH, FFN_HIDDEN, D_MODEL), FFN_HIDDEN ** -0.5),
    }

def reference(x_prompt, x_sample, state_hgrn, state_gla, cache_fox_k, cache_fox_v, cache_fox_logf,
              cache_dsa_k, cache_dsa_v, cache_dsa_ik, norm_mix, norm_ffn, norm_final, ab_w_in, ab_w_out,
              hgrn_lb_logits, hgrn_gnorm, gla_w_gk, gla_b_gk, gla_gnorm, cd_w_in, cd_w_out, fox_f_bias,
              ffn_w_in, ffn_w_out):
    weights = (norm_mix, norm_ffn, norm_final, ab_w_in, ab_w_out, hgrn_lb_logits, hgrn_gnorm, gla_w_gk,
               gla_b_gk, gla_gnorm, cd_w_in, cd_w_out, fox_f_bias, ffn_w_in, ffn_w_out)
    bp = x_prompt.shape[0]
    zero_hgrn = jnp.zeros((N_AB, bp, A_HEADS, A_DK, A_DV), F32)
    zero_gla = jnp.zeros((N_AB, bp, B_HEADS, B_DK, B_DV), F32)
    (y_prompt, p_hgrn, p_gla, p_fox_k, p_fox_v, p_fox_logf, p_dsa_k, p_dsa_v, p_dsa_ik) = run_trunk(
        x_prompt, zero_hgrn, zero_gla, None, *weights)
    cd_cache = (cache_fox_k, cache_fox_v, cache_fox_logf, cache_dsa_k, cache_dsa_v, cache_dsa_ik)
    (y_sample, s_hgrn, s_gla, s_fox_k, s_fox_v, s_fox_logf, s_dsa_k, s_dsa_v, s_dsa_ik) = run_trunk(
        x_sample, state_hgrn, state_gla, cd_cache, *weights)
    return (y_prompt, y_sample, p_hgrn, p_gla, p_fox_k, p_fox_v, p_fox_logf, p_dsa_k, p_dsa_v, p_dsa_ik,
            s_hgrn, s_gla, s_fox_k, s_fox_v, s_fox_logf, s_dsa_k, s_dsa_v, s_dsa_ik)


_drawn_inputs = setup_inputs


def setup_inputs(seed=0):
    import zlib

    import numpy as np

    out = dict(_drawn_inputs(seed))
    spreads = {}
    factors = {}
    for name, (base, spread) in spreads.items():
        noise = np.random.default_rng([zlib.crc32(name.encode()), seed]).standard_normal(out[name].shape)
        drawn = base * np.exp(spread * noise) if base else spread * noise
        out[name] = __import__('jax').numpy.asarray(drawn.astype(out[name].dtype))
    for name, factor in factors.items():
        out[name] = (out[name] * factor).astype(out[name].dtype)
    return out
```

```python
from contextlib import ExitStack

import concourse.bass as bass
from concourse import mybir

ALU = mybir.AluOpType
ACT = mybir.ActivationFunctionType
F32 = mybir.dt.float32
F32R = mybir.dt.float32r
BF16 = mybir.dt.bfloat16
U32 = mybir.dt.uint32
AX_X = mybir.AxisListType.X

P = 128
SLOTS = 4
LEAD = 2


class Chain:

    def __init__(self, eng, sem):
        self.eng, self.sem, self.n = eng, sem, 0

    def add(self, ins):
        ins.then_inc(self.sem, 1)
        self.n = self.n + 1
        return self.n

    def link(self, ins):
        self.add(ins)
        self.eng.wait_ge(self.sem, self.n)


def build(nc, I, O):
    D = I["x_prompt"].shape[2]
    TP = I["x_prompt"].shape[1]
    TS = I["x_sample"].shape[1]
    T = TP + TS
    KT = D // P
    NT = TP // P
    HALF = T // 2
    AH, ADK, ADV = I["state_hgrn"].shape[2:]
    BH, BDK, BDV = I["state_gla"].shape[2:]
    PAST, CH, HD = I["cache_fox_k"].shape[2:]
    DKV = I["cache_dsa_k"].shape[3]
    IDX = I["cache_dsa_ik"].shape[3]
    RANK = I["gla_w_gk"].shape[1]
    FH = I["ffn_w_out"].shape[1]
    FT = FH // P
    PART = 8
    BLK = 32
    MID = BLK // 2 - 1
    NB = TP // BLK
    CHUNK = 64
    KS = PAST + TS
    TOPP = min(256, TP // 4)
    TOPS = min(256, KS // 4)
    DH = 8
    EPS = 1e-6
    NEG = -1e30
    TAKEN = -3e38
    EW = 1024
    assert T == (NB + 1) * BLK and TS == BLK and D == 1024 and ADK == ADV == BDV == P and BDK == 64
    assert FT == 22 and TOPP == P and HD == IDX == 64 and CH == 8 and DKV == 2

    w_ab = I["ab_w_in"][0].rearrange("(k p) n -> p k n", p=P)
    w_cd = I["cd_w_in"][0].rearrange("(k p) n -> p k n", p=P)
    w_abo = I["ab_w_out"][0].rearrange("(k p) n -> p k n", p=P)
    w_cdo = I["cd_w_out"][0]
    w_f1 = [I["ffn_w_in"][l].rearrange("(k p) n -> p k n", p=P) for l in range(2)]
    w_f2 = [I["ffn_w_out"][l].rearrange("(k p) n -> p k n", p=P) for l in range(2)]
    AQ, AF, AI, AG = 0, AH * ADK, 2 * AH * ADK, 3 * AH * ADK
    BQ = AG + AH * ADV
    BK, BV = BQ + BH * BDK, BQ + 2 * BH * BDK
    BG = BV + BH * BDV
    BLR = BG + BH * BDV
    CQ, CK, CV = 0, CH * HD, 2 * CH * HD
    CF = 3 * CH * HD
    DQ = CF + CH
    DK = DQ + DH * HD
    TB = DK + DKV * HD
    TBW = DKV * HD + 4 * IDX + IDX + 4
    OIQ, OIK, OIW = DKV * HD, DKV * HD + 4 * IDX, DKV * HD + 5 * IDX

    plan = []
    whole = slice(0, P)

    def cols(w, k0, kn, c0, n):
        return [(whole, (kn, n), slice(0, kn), w[:, k0:k0 + kn, c0:c0 + n])]

    def section(w, c0, n):
        for k in range(0, KT, 2):
            plan.append(cols(w, k, 2, c0, n))

    units = [("b", t) for t in range(BH // 2)] + [("a", u) for u in range(AH)]
    NU = len(units)
    section(w_ab, AI, AH * ADV)
    C_LR = len(plan)
    plan.append(cols(w_ab, 0, KT, BLR, RANK))
    order = [("x", k) for k in range(KT)] + [0, C_LR]
    c_key, c_query, c_gates = [], [], [[] for _ in units]

    def unit_chunk(chunks, c0):
        chunks.append(len(plan))
        order.append(len(plan))
        plan.append(cols(w_ab, 0, KT, c0, P))

    def plan_key(u):
        if u < NU:
            kind, i = units[u]
            if kind == "b":
                order.append(("gk", u))
            unit_chunk(c_key, (AF if kind == "a" else BK) + i * P)

    def plan_query(u):
        if u < NU:
            kind, i = units[u]
            unit_chunk(c_query, (AQ if kind == "a" else BQ) + i * P)

    plan_key(0)
    plan_query(0)
    C_BV = len(plan)
    section(w_ab, BV, BH * BDV)
    order.append(C_BV)
    for u, (kind, i) in enumerate(units):
        if kind == "b":
            order.append(("score", u))
        plan_key(u + 1)
        plan_query(u + 1)
        for e, c0 in enumerate([AG + i * P] if kind == "a" else [BG + 2 * i * P, BG + (2 * i + 1) * P]):
            unit_chunk(c_gates[u], c0)
            order.append(("sum", u, e))
    C_O0 = len(plan)
    for m in range(KT):
        plan.append(cols(w_abo, 0, KT, m * P, P))
    C_F = [len(plan), 0]

    def ffn_chunks(l):
        for r in range(0, FT, PART):
            n = min(PART, FT - r)
            for j in range(r, r + n):
                plan.append(cols(w_f1[l], 0, KT, j * P, P))
                plan.append(cols(w_f1[l], 0, KT, FH + j * P, P))
            for m in range(KT):
                plan.append(cols(w_f2[l], r, n, m * P, P))

    ffn_chunks(0)
    C_M1 = len(plan)
    section(w_cd, TB, TBW)
    C_CF = len(plan)
    plan.append(cols(w_cd, 0, KT, CF, CH))
    C_CK = [C_CF + 1 + t for t in range(4)]
    for t in range(4):
        plan.append(cols(w_cd, 0, KT, CK + t * P, P))
    C_CQ = []
    for t in range(4):
        if t == 2:
            C_CV = len(plan)
            section(w_cd, CV, CH * HD)
        C_CQ.append(len(plan))
        plan.append(cols(w_cd, 0, KT, CQ + t * P, P))
    C_DK = len(plan)
    plan.append(cols(w_cd, 0, KT, DK, DKV * HD))
    C_DQ = [C_DK + 1 + t for t in range(4)]
    for t in range(4):
        plan.append([(whole, (KT, P), (slice(0, KT), slice(g * HD, g * HD + HD)),
                      w_cd[:, :, DQ + (4 * g + t) * HD:DQ + (4 * g + t + 1) * HD]) for g in range(2)])
    C_O1 = len(plan)
    for m in range(KT):
        ch = [(whole, (KT, P), slice(0, 4), w_cdo[0:4 * P, m * P:(m + 1) * P].rearrange("(k p) n -> p k n", p=P))]
        for g in range(2):
            r0 = 4 * P + g * 4 * HD
            ch.append((slice(g * HD, g * HD + HD), (KT, P), slice(4, 8),
                       w_cdo[r0:r0 + 4 * HD, m * P:(m + 1) * P].rearrange("(k p) n -> p k n", p=HD)))
        plan.append(ch)
    C_F[1] = len(plan)
    ffn_chunks(1)
    C_END = len(plan)
    landed = []
    use = [0] * SLOTS
    for c, ch in enumerate(plan):
        use[c % SLOTS] += 16 * len(ch)
        landed.append(use[c % SLOTS])

    order += [c for c in range(C_O0, C_END) if not (C_M1 < c < C_M1 + 4 or C_CV < c < C_CV + 4)]
    order.insert(order.index(C_M1) + 1, "norm")
    jof = {key: j for j, key in enumerate(order)}
    for c0 in (0, C_BV, C_M1, C_CV):
        for c in range(c0 + 1, c0 + 4):
            jof[c] = jof[c0]

    with ExitStack() as ctx:
        def sb(name, shape, dt=F32):
            return ctx.enter_context(nc.sbuf_tensor(name, shape, dt))

        sems = {}

        def sem(name):
            if name not in sems:
                sems[name] = ctx.enter_context(nc.semaphore(name))
            return sems[name]

        xT = sb("xT", [P, KT, T])
        xh, xl = sb("x_hi", [P, KT, T], F32R), sb("x_lo", [P, KT, T], F32R)
        oh, ol = sb("o_hi", [P, KT, T], F32R), sb("o_lo", [P, KT, T], F32R)
        raw = sb("w_raw", [P, SLOTS, EW])
        wh, wl = sb("w_hi", [P, SLOTS, EW], F32R), sb("w_lo", [P, SLOTS, EW], F32R)
        ident = sb("ident", [P, P])
        identb = sb("identb", [P, P], BF16)
        ones = sb("ones", [P, P])
        par = sb("par", [P, 64])
        small = sb("small", [P, 128])
        AR = 17408
        arena = sb("arena", [P, AR])
        ps = ctx.enter_context(nc.psum_tensor("ps", [P, 8, 512], F32))
        used = [0]

        def area(n):
            used[0] += n
            assert used[0] <= AR, used[0]
            return arena[:, used[0] - n:used[0]]

        raw_landed = [sem(f"raw_landed{s}") for s in range(SLOTS)]
        hi_done, lo_done, chunk_done = sem("hi_done"), sem("lo_done"), sem("chunk_done")
        job_done = sem("job_done")
        pair_free = [sem("pair_free0"), sem("pair_free1")]
        dve_s, act_s, pe_s, pool_s = sem("dve_s"), sem("act_s"), sem("pe_s"), sem("pool_s")
        s_in, s_par, s_const = sem("s_in"), sem("s_par"), sem("s_const")
        s_part = sem("s_part")
        s_sq, s_ss, s_rs, s_nt, s_nh, s_nl = (sem(n) for n in ("sq_done", "ss_done", "rstd_done", "norm_done", "norm_hi", "norm_lo"))
        f_sig, f_mul, f_hi, f_lo = sem("f_sig"), sem("f_mul"), sem("f_hi"), sem("f_lo")
        s_acc, s_rt, x_scaled, k_scaled = sem("squares_added"), sem("rcol_done"), sem("x_scaled"), sem("k_scaled")
        o_hi, o_lo = sem("o_hi"), sem("o_lo")
        x_turned, y_turned, y_ready = sem("x_turned"), sem("y_turned"), sem("y_ready")
        s_out = sem("s_out")

        rows, prow = [], {}
        for name, src, n in [("mix0", I["norm_mix"][0], 8), ("mix1", I["norm_mix"][1], 8), ("ffn0", I["norm_ffn"][0], 8),
                             ("ffn1", I["norm_ffn"][1], 8), ("final", I["norm_final"], 8),
                             ("lb0", I["hgrn_lb_logits"][0], 4), ("lb1", I["hgrn_lb_logits"][1], 4),
                             ("ga", I["hgrn_gnorm"][0], 1), ("gb", I["gla_gnorm"][0], 1), ("bgk", I["gla_b_gk"][0], 2)]:
            prow[name] = sum(r[1] for r in rows)
            rows.append((src.rearrange("(k p) -> k p", p=P), n))
        NPR = sum(r[1] for r in rows)

        def pc(name, k=0):
            return par[:, prow[name] + k:prow[name] + k + 1]

        eps_c = small[:, 0:1]
        norm_names = ["mix0", "ffn0", "mix1", "ffn1", "final"]

        x_in = arena[:, 0:NT * D].rearrange("p (i d) -> p i d", i=NT)
        xs_in = arena[0:TS, NT * D:(NT + 1) * D]
        par_in = arena[0:NPR, 6000:6000 + P]
        NR = 4
        nsq = arena[:, AR - NR * T:AR].rearrange("p (r t) -> p r t", r=NR)
        ntmp = nsq
        acc, sq2 = nsq[:, NR - 1, :], nsq[:, 1:NR - 1, :]
        rstd = sb("rstd", [P, T])[:, :]
        rcol = small[:, 44:44 + NT + 1]
        x_out = arena[:, 6000:6000 + KT * T].rearrange("p (k t) -> p k t", k=KT)
        y_sb = arena[:, 0:(NT + 1) * D].rearrange("p (i d) -> p i d", i=NT + 1)
        fsig = arena[:, 0:2 * T].rearrange("p (r t) -> p r t", r=2)
        fh = arena[:, 2 * T:4 * T].rearrange("p (r t) -> p r t", r=2)
        fg = arena[:, 4 * T:6 * T].rearrange("p (r t) -> p r t", r=2)

        def pair(c):
            b = 2 * (jof[c] % 2)
            return ps[:, b:b + 2, 0:HALF]

        def wait_done(eng, c, it=0):
            eng.wait_ge(chunk_done, c + 1 + 4 * it)

        def frees(c):
            return pair_free[jof[c] % 2]

        def wait_freed(eng, c, it=0):
            eng.wait_ge(frees(c), jof[c] // 2 + 1 + 2 * it)

        def two(ap):
            return ap.rearrange("p (h t) -> p h t", h=2)


        used[0] = 0
        val = area((NT + 1) * D).rearrange("p (i d) -> p i d", i=NT + 1)
        qp = area(2 * T).rearrange("p (r t) -> p r t", r=2)
        kp = area(2 * T).rearrange("p (r t) -> p r t", r=2)
        q2 = area(2 * T).rearrange("p (r t) -> p r t", r=2)
        s0h = area(AH * ADV).rearrange("p (h v) -> p h v", h=AH)
        s0g = area(BH // 2 * BDV).rearrange("p (h v) -> p h v", h=BH // 2)
        att = area(2 * T).rearrange("p (r t) -> p r t", r=2)
        gate = area(2 * T).rearrange("p (r t) -> p r t", r=2)
        ktm = area((NT + 1) * P).rearrange("p (i k) -> p i k", i=NT + 1)
        rst = area((NB + 1) * ADV).rearrange("p (n v) -> p n v", n=NB + 1)
        t1, t2, t3, t4 = (area(T) for _ in range(4))
        osb, osq = area(T), area(T)
        lrT = rstd[0:RANK, :]
        smask = sb("smask", [P, T], BF16)
        matt = sb("matt", [P, P])
        cm = small[:, 1:25]
        lb, oml = small[:, 25:29], small[:, 29:33]
        tail_, ee = small[:, 33:33 + NB + 1], small[:, 50:50 + NB + 1]
        ex = [small[:, 67 + 17 * r:84 + 17 * r] for r in range(2)]
        tx = sb("tx", [P, 2, NB + 1])
        wgk = sb("wgk", [RANK, BH * BDK])
        s_m0in, s_m0c, gk_done, u_act, u_dve = (sem(n) for n in ("m0_in", "m0_const", "gk_done", "unit_act", "unit_dve"))
        s_val, s_lb, gate_sig, q_decayed, state_final, att_parts = (sem(n) for n in (
            "val_done", "lb_done", "gate_sig", "q_decayed", "state_final", "att_parts"))
        r_kt, r_ktm, r_att, r_attm, r_w, r_r, r_o, r_osb, r_oss, r_ors, r_on, m0_out = (sem(n) for n in (
            "keys_turned", "keys_copied", "att_done", "att_masked", "update_done", "state_done", "o_done", "o_squared",
            "o_sum", "o_rstd", "o_gated", "m0_out"))

        def unit(u):
            kind, i = units[u]
            if kind == "a":
                return kind, i, [(0, P, i * ADV, i)], s0h[:, i, :]
            return kind, i, [(e * BDK, BDK, (AH + 2 * i + e) * ADV, AH + 2 * i + e) for e in range(2)], s0g[:, i, :]

        heads_before, UD, UA = ([sum(n[kind] for kind, _ in units[:u]) for u in range(NU + 1)]
                                for n in ({"a": 1, "b": 2}, {"a": 9, "b": 7}, {"a": 6, "b": 5}))
        PRE = {"a": 2, "b": 1}
        split = [(0, 0, 2 * P), (1, 2 * P, T)]

        NW = 5

        def obank(e):
            return 6 - 2 * e

        def last(u):
            return len(c_gates[u]) - 1

        used[0] = 0
        by_tile = lambda ap, k: ap.rearrange("p (k t) -> p k t", k=k)
        q_area = area(4 * T)
        qT = by_tile(q_area, 4)
        W = TP + KS
        lf, lf_a, lf_z, lf_cum = q_area[0:CH, 0:W], q_area[0:CH, W:W + T], q_area[0:CH, W + T:W + 2 * T], q_area[0:CH, W + T:2 * W + T]
        pt_at = used[0]
        nks = [2 * P, 3 * P, 4 * P, KS]
        idx = [area(n) for n in nks]
        pt = arena[:, pt_at:pt_at + 1024].rearrange("p (r k) -> p r k", r=2)
        kT = by_tile(area(4 * T), 4)
        v_area = area((NT + 1) * CH * HD)
        cv = v_area.rearrange("p (i n) -> p i n", i=NT + 1)
        ck_raw = v_area[:, 0:1024].rearrange("p (i n) -> p i n", i=2)
        dk_raw = v_area[:, 1024:1280].rearrange("p (i n) -> p i n", i=2)
        ik_raw = v_area[:, 1280:1536].rearrange("p (i n) -> p i n", i=2)
        lf_raw = v_area[:, 1536:1552].rearrange("p (i n) -> p i n", i=2)
        relu = v_area[:, 0:2048].rearrange("p (h k) -> p h k", h=4)
        ckc = area(4 * PAST).rearrange("p (t k) -> p t k", t=4)
        cvc = area(2 * CH * HD).rearrange("p (i n) -> p i n", i=2)
        dv = area((NT + 1) * P).rearrange("p (i n) -> p i n", i=NT + 1)
        dkc = area(PAST)
        dvc = area(2 * P).rearrange("p (i n) -> p i n", i=2)
        mb_all = area(784).bitcast(BF16)
        mb_off = [0, P, 3 * P, 6 * P, 10 * P]
        mb = [mb_all[:, o:o + n] for o, n in zip(mb_off, [P] + nks)]
        caus = area(P // 2).bitcast(BF16)
        sel = area(CH * P // 2).bitcast(BF16).rearrange("p (h m) -> p h m", h=CH)
        cp = area(W // 2).bitcast(BF16)
        x_area = area(4096)
        ikc = x_area[:, 0:PAST]
        iqT = by_tile(x_area[:, PAST:PAST + 2 * T], 2)
        ikT = x_area[:, PAST + 2 * T:PAST + 3 * T]
        SW = TBW - DKV * HD
        stage = x_area[:, PAST + 3 * T:PAST + 3 * T + (NT + 1) * SW].rearrange("p (i n) -> p i n", i=NT + 1)
        lft = x_area[:, 3508:3508 + (NT + 1) * CH].rearrange("p (i n) -> p i n", i=NT + 1)
        prob = x_area[:, 0:1536].rearrange("p (r k) -> p r k", r=3)
        k_out = x_area[:, 1536:4096].rearrange("p (i n) -> p i n", i=NT + 1)
        m8 = small[:, 1:9]
        mx, nmx, psums, rec = (small[:, 9 + 8 * n:17 + 8 * n].rearrange("p (r j) -> p r j", j=2) for n in range(4))
        fb = small[0:CH, 41:42]
        s_m1in, s_m1c, c_turned, c_out, m1_out = (sem(n) for n in ("m1_in", "m1_const", "cache_turned", "cache_taken", "m1_out"))
        tb_out, i_turned, i_out, lf_abs, lf_ready, lf_turned, lf_out, cp_done = (sem(n) for n in (
            "tb_taken", "idx_turned", "idx_taken", "lf_abs", "lf_ready", "lf_turned", "lf_taken", "cp_done"))
        sc_done, sc_relu, sc_acc, cv_out, k_turned, k_taken = (sem(n) for n in (
            "score_done", "score_relu", "score_added", "cv_taken", "k_turned", "k_taken"))
        at_m, at_l, at_mx, at_e, at_p, at_t, at_c, at_v, at_h, at_o = (sem(n) for n in (
            "att_masks", "att_logits", "att_max", "att_exp", "att_probs", "att_turned", "att_copied", "att_values",
            "att_hi", "att_lo"))
        N_M0_OUT = sum(2 * (1 if kind == "a" else 2) for kind, _ in units)

        groups = [(2 * t + e, tiles) for t in range(4) for e in range(2)
                  for tiles in ([(0, 0, P), (1, P, 2 * P)], [(2, 0, 3 * P)], [(3, 0, 4 * P)])]
        groups += [(w, None) for w in range(2)]
        NX = len(groups)
        pairs_end = [6 * (t + 1) - 1 for t in range(4)] + [NX - 1]
        block = ctx.enter_context(nc.Block())

        @block.sync
        def _(sp):
            def load(c, it=0, at=None):
                if c >= SLOTS or not isinstance(it, int):
                    sp.wait_ge(lo_done, c - SLOTS + 1 + 4 * it)
                for parts, shape, sub, src in plan[c]:
                    v = raw[parts, c % SLOTS, 0:shape[0] * shape[1]].rearrange("p (k n) -> p k n", k=shape[0])
                    v = v[:, sub, :] if isinstance(sub, slice) else v[:, sub[0], sub[1]]
                    sp.dma_start(v, src if at is None else at).then_inc(raw_landed[c % SLOTS], 16)

            def ffn_part(l, cb, itp, r0, n):
                with sp.Fori(0, n // 2) as i:
                    for k in range(4):
                        load(cb + k, itp + i, w_f1[l][:, :, bass.ds((i * 2 + k // 2 + r0) * P + (k % 2) * FH, P)])
                with sp.Fori(0, 2) as i:
                    for k in range(4):
                        load(cb + 2 * n + k, itp + i, w_f2[l][:, bass.ds(r0, n), bass.ds((i * 4 + k) * P, P)])

            def ffn(l):
                with sp.Fori(0, 2) as part:
                    ffn_part(l, C_F[l], part * 6, part * PART, PART)
                ffn_part(l, C_F[l] + 48, 0, 2 * PART, FT - 2 * PART)

            off = 0
            for src, n in rows:
                sp.dma_start(par_in[off:off + n, :], src).then_inc(s_par, 16)
                off += n
            for i in range(NT):
                sp.dma_start(x_in[:, i, :], I["x_prompt"][0, i * P:(i + 1) * P, :]).then_inc(s_in, 16)
            sp.dma_start(xs_in, I["x_sample"][0]).then_inc(s_in, 16)
            for c in range(SLOTS):
                load(c)
            sp.dma_start(s0h, I["state_hgrn"][0, 0].rearrange("h k v -> k h v")).then_inc(s_m0in, 16)
            for e in range(2):
                sp.dma_start(s0g[e * BDK:(e + 1) * BDK], I["state_gla"][0, 0].rearrange("(i e) k v -> e k i v", e=2)[e]).then_inc(s_m0in, 16)
            sp.dma_start(wgk[:, :], I["gla_w_gk"][0]).then_inc(s_m0in, 16)
            for c in range(SLOTS, C_F[0]):
                load(c)
            sp.wait_ge(m0_out, 16 * N_M0_OUT)
            for dst, name in ((ck_raw, "fox_k"), (cvc, "fox_v"), (dk_raw, "dsa_k"), (dvc, "dsa_v")):
                sp.dma_start(dst, I["cache_" + name][0, 0].rearrange("(i p) h n -> p i (h n)", p=P)).then_inc(s_m1in, 16)
            for e in range(2):
                sp.dma_start(ik_raw[:, :, e * IDX:(e + 1) * IDX], I["cache_dsa_ik"][0, 0].rearrange("(i p) n -> p i n", p=P)).then_inc(s_m1in, 16)
            sp.dma_start(lf_raw, I["cache_fox_logf"][0, 0].rearrange("(i p) n -> p i n", p=P)).then_inc(s_m1in, 16)
            sp.dma_start(fb, I["fox_f_bias"][0].rearrange("(h o) -> h o", o=1)).then_inc(s_m1in, 16)
            ffn(0)
            for c in range(C_M1, C_F[1]):
                load(c)
            ffn(1)
            for i in range(NT + 1):
                sp.wait_ge(y_ready, i + 1)
                dst = O["y_prompt"][0, i * P:(i + 1) * P, :] if i < NT else O["y_sample"][0]
                sp.dma_start(dst, y_sb[0:P if i < NT else TS, i, :]).then_inc(s_out, 16)
            sp.wait_ge(s_out, 16 * (NT + 1))
            sp.wait_ge(m0_out, 16 * N_M0_OUT)
            sp.wait_ge(m1_out, 16 * 12)

        @block.gpsimd
        def _(pool):
            ch = Chain(pool, pool_s)
            ch.add(pool.memset(ident[:, :], 0.0))
            ch.add(pool.memset(identb[:, :], 0.0))
            ch.add(pool.memset(small[:, :], 0.0))
            ch.link(pool.memset(ones[:, :], 1.0))
            for t in (ident, identb):
                pool.affine_select(out=t[:, :], in_=t[:, :], compare_op=ALU.not_equal, fill=1.0, base=0,
                                   pattern=[[-1, P]], channel_multiplier=1).then_inc(s_const, 1)
            pool.memset(eps_c, EPS).then_inc(s_const, 1)

            def lo(c, it=0):
                pool.wait_ge(hi_done, c + 1 + 4 * it)
                s = c % SLOTS
                pool.tensor_tensor(wl[:, s, :], raw[:, s, :], wh[:, s, :].bitcast(F32), ALU.subtract).then_inc(lo_done, 1)

            def los(c0, c1):
                with pool.Fori(0, (c1 - c0) // 4) as i:
                    for k in range(4):
                        lo(c0 + k, i)
                for c in range(c0 + (c1 - c0) // 4 * 4, c1):
                    lo(c)

            ch.add(pool.memset(smask[:, :], 1.0))
            ch.link(pool.memset(matt[:, :], 1.0))
            pool.memset(smask[:, 0:T:BLK], 0.0).then_inc(s_m0c, 1)
            ch.link(pool.affine_select(out=matt[:, :], in_=matt[:, :], compare_op=ALU.is_ge, fill=0.0, base=0,
                                       pattern=[[1, P]], channel_multiplier=-1))
            mv = matt[:, :].rearrange("p (b l) -> p b l", l=BLK)
            pool.affine_select(out=mv, in_=mv, compare_op=ALU.is_ge, fill=0.0, base=0,
                               pattern=[[-BLK, P // BLK], [0, BLK]], channel_multiplier=1).then_inc(s_m0c, 1)
            los(0, C_F[0] + PART)
            pool.wait_ge(m0_out, 16 * N_M0_OUT)
            ch.add(pool.memset(cp[0:96, :], 0.0))
            ch.add(pool.memset(sel[0:96], 0.0))
            ch.add(pool.memset(caus, 0.0))
            ch.link(pool.memset(mb[0], 0.0))
            pool.affine_select(out=caus, in_=caus, compare_op=ALU.is_ge, fill=NEG, base=0, pattern=[[-1, P]], channel_multiplier=1)\
                .then_inc(s_m1c, 1)
            pool.memset(mb[0][0:CHUNK, CHUNK:P], NEG).then_inc(s_m1c, 1)
            for b in range(3):
                ins = pool.affine_select(out=sel[0:96], in_=sel[0:96], compare_op=ALU.not_equal, fill=1.0, base=-32 * b,
                                         pattern=[[-1, CH], [0, P]], channel_multiplier=1)
                if b < 2:
                    ch.link(ins)
                else:
                    ins.then_inc(s_m1c, 1)
            los(C_F[0] + PART, C_M1)
            for c in range(C_M1, C_O1):
                lo(c)
                if c - LEAD in C_CK + C_CQ:
                    k = c - LEAD
                    tile = kT[:, C_CK.index(k), :] if k in C_CK else qT[:, C_CQ.index(k), :]
                    wait_freed(pool, k)
                    pool.tensor_tensor(tile, tile, rstd[:, :], ALU.mult).then_inc(k_scaled, 1)
            los(C_O1, C_END)

        @block.scalar
        def _(act):
            ch = Chain(act, act_s)

            def hi(c, it=0):
                if isinstance(it, int) and c >= C_END:
                    return
                s = c % SLOTS
                act.wait_ge(raw_landed[s], landed[c] + 16 * it)
                if c >= SLOTS:
                    wait_done(act, c - SLOTS, it)
                act.activation(wh[:, s, :], raw[:, s, :], ACT.Copy).then_inc(hi_done, 1)

            def first_norm():
                for k in range(KT):
                    act.wait_ge(pair_free[k % 2], k // 2 + 1)
                    if k >= NR:
                        act.wait_ge(s_ss, k - NR + 1)
                    act.activation(nsq[:, k % NR, :], xT[:, k, :], ACT.Square).then_inc(s_sq, 1)
                rms(0)
                for k in range(KT):
                    act.wait_ge(s_nt, k + 1)
                    act.activation(xh[:, k, :], ntmp[:, k % NR, :], ACT.Copy).then_inc(s_nh, 1)

            def rms(n, b=6):
                act.wait_ge(s_ss, KT + n)
                act.wait_ge(s_const, 3)
                if n < 4:
                    ch.link(act.activation(two(rstd), ps[:, b:b + 2, 0:HALF], ACT.Ln, bias=eps_c, scale=1.0 / D))
                    act.activation(rstd, rstd, ACT.Exp, scale=-0.5).then_inc(s_rs, 1)
                if n in (2, 4):
                    cols = ((P, 0, NT), (TS, NT, NT + 1))
                    for m, i0, i1 in cols:
                        ins = act.activation(rcol[0:m, i0:i1], ps[0:m, b, HALF + i0:HALF + i1], ACT.Ln, bias=eps_c[0:m], scale=1.0 / D)
                    ins.then_inc(frees("norm") if n == 2 else s_rt, 1)
                    if n == 2:
                        wait_freed(act, "norm")
                    else:
                        act.wait_ge(s_rt, 2)
                    for m, i0, i1 in cols:
                        ins = act.activation(rcol[0:m, i0:i1], rcol[0:m, i0:i1], ACT.Exp, scale=-0.5)
                    ins.then_inc(s_rt, 1)
                    act.wait_ge(s_rt, 1 if n == 2 else 3)

            def next_x(n, c0, m):
                wait_freed(act, c0 + m)
                if n < 4:
                    act.activation(xh[:, m, :], xT[:, m, :], ACT.Copy, scale=pc(norm_names[n], m)).then_inc(s_nh, 1)
                if m >= 3:
                    act.wait_ge(s_acc, (KT - 1) * (n - 1) + m - 2)
                act.activation(acc if m == 0 else sq2[:, m % 2, :], xT[:, m, :], ACT.Square).then_inc(s_sq, 1)

            def ffn_part(l, cb, itp, hx, n, last=False):
                with act.Fori(0, n // 2) as i:
                    it = itp + i
                    for k in range(4):
                        hi(cb + k + LEAD, it)
                        if k % 2 == 0:
                            wait_freed(act, cb + k, it)
                            act.activation(fsig[:, k // 2, :], fg[:, k // 2, :], ACT.Sigmoid).then_inc(f_sig, 1)
                        else:
                            wait_freed(act, cb + k, it)
                            act.activation(oh[:, bass.ds(i * 2 + k // 2, 1), :], fh[:, k // 2:k // 2 + 1, :],
                                           ACT.Copy).then_inc(f_hi, 1)
                if last:
                    for k in range(KT):
                        hi(cb + 2 * n + k + LEAD)
                        next_x(2 * l + 2, cb + 2 * n, k)
                else:
                    with act.Fori(0, 2) as i:
                        for k in range(4):
                            hi(cb + 2 * n + k + LEAD, itp + i)

            def ffn(l):
                with act.Fori(0, 2) as part:
                    ffn_part(l, C_F[l], part * 6, part * PART, PART)
                ffn_part(l, C_F[l] + 48, 0, 0, FT - 2 * PART, last=True)

            for c in range(LEAD):
                hi(c)
            first_norm()
            hp = [LEAD]

            def ahead(c):
                while hp[0] <= c + LEAD:
                    hi(hp[0])
                    hp[0] += 1

            def key_gates(u):
                kind, i, hs, s0 = unit(u)
                c0, d0 = c_key[u], UD[u]
                ahead(c0)
                act.wait_ge(u_dve, d0)
                if kind == "a":
                    wait_done(act, c0)
                    act.activation(two(t1), pair(c0), ACT.Sigmoid).then_inc(frees(c0), 1)
                    act.wait_ge(u_dve, d0 + 2)
                    act.activation(t2, t2, ACT.Ln).then_inc(u_act, 1)
                else:
                    act.wait_ge(gk_done, i + 1)
                    ch.link(act.activation(two(t1), pair(("gk", u)), ACT.Abs, bias=pc("bgk", i)))
                    ch.link(act.activation(t1, t1, ACT.Exp, scale=-1.0))
                    act.activation(t1, t1, ACT.Ln, bias=ones[:, 0:1]).then_inc(u_act, 1)

            def decays(u):
                kind, a0, d0 = units[u][0], UA[u], UD[u]
                scale = 1.0 if kind == "a" else 1.0 / 16.0
                act.wait_ge(u_dve, d0 + PRE[kind] + 5)
                act.activation(ex[u % 2], ee, ACT.Exp, scale=scale).then_inc(u_act, 1)
                act.activation(tx[:, u % 2, :], tail_, ACT.Exp, scale=scale).then_inc(u_act, 1)
                act.activation(t3, t2, ACT.Exp, scale=scale).then_inc(u_act, 1)
                act.wait_ge(u_act, a0 + 4)
                act.activation(t2, t2, ACT.Exp, scale=-scale).then_inc(u_act, 1)

            def query_gate(u):
                ahead(c_query[u])
                if units[u][0] == "a":
                    wait_done(act, c_query[u])
                    act.activation(two(t4), pair(c_query[u]), ACT.Sigmoid).then_inc(u_act, 1)

            def out_gate(u, e):
                c = c_gates[u][e]
                ahead(c)
                act.wait_ge(o_lo, heads_before[u])
                wait_done(act, c)
                act.activation(two(gate[:, e, :]), pair(c), ACT.Sigmoid).then_inc(gate_sig, 1)

            def turned_keys(u):
                act.wait_ge(r_kt, u + 1)
                if u > 0:
                    act.wait_ge(r_w, NW * u)
                for b in range(2):
                    act.activation(ktm[:, 2 * b:2 * b + 2, :], ps[:, 4 + b, 0:2 * P].rearrange("p (i k) -> p i k", k=P), ACT.Copy)\
                       .then_inc(r_ktm, 1)
                act.activation(ktm[0:TS, NT, :], ps[0:TS, 5, 2 * P:3 * P], ACT.Copy).then_inc(r_ktm, 1)

            def states(u):
                kind, i, hs, s0 = unit(u)
                act.wait_ge(state_final, 2 * (u + 1))
                for ko, kz, vc, hd in hs:
                    for out, n in (("p_", NB - 1), ("s_", NB)):
                        dst = O[out + "hgrn"][0, 0, hd] if kind == "a" else O[out + "gla"][0, 0, hd - AH]
                        act.dma_start(dst, rst[ko:ko + kz, n, :]).then_inc(m0_out, 16)

            def head_out(u, e):
                h = heads_before[u] + e
                act.wait_ge(r_o, h + 1)
                act.wait_ge(o_lo, h)
                for b, n0, n1 in split:
                    ch.link(act.activation(osb[:, n0:n1], ps[:, obank(e) + b, 0:n1 - n0], ACT.Copy))
                act.activation(osq, osb, ACT.Square).then_inc(r_osb, 1)

            def head_rms(u, e):
                h, key = heads_before[u] + e, ("sum", u, e)
                act.wait_ge(r_oss, h + 1)
                act.activation(two(osq), pair(key), ACT.Ln, bias=eps_c, scale=1.0 / ADV).then_inc(frees(key), 1)
                wait_freed(act, key)
                act.activation(osq, osq, ACT.Exp, scale=-0.5).then_inc(r_ors, 1)

            def head_hi(u, e):
                h = heads_before[u] + e
                act.wait_ge(r_on, h + 1)
                act.activation(oh[:, unit(u)[2][e][3], :], osb, ACT.Copy).then_inc(o_hi, 1)

            def take_values(c0, v0):
                for c in range(c0, c0 + 4):
                    ahead(c)
                wait_done(act, c0 + 3)
                for i in range(NT):
                    act.activation(val[:, i, v0:v0 + 512], ps[:, 4 + i, :], ACT.Copy).then_inc(s_val, 1)
                act.activation(val[0:TS, NT, v0:v0 + 512], ps[0:TS, 2 * (jof[c0] % 2), :], ACT.Copy).then_inc(frees(c0), 1)

            act.wait_ge(s_lb, 2)
            act.activation(cm[:, 4:12], cm[:, 4:12], ACT.Exp).then_inc(s_lb, 1)
            take_values(0, 0)
            ahead(C_LR)
            wait_done(act, C_LR)
            jl = 2 * (jof[C_LR] % 2)
            act.activation(two(lrT), ps[0:RANK, jl:jl + 2, 0:HALF], ACT.Copy).then_inc(frees(C_LR), 1)
            key_gates(0)
            decays(0)
            query_gate(0)
            take_values(C_BV, AH * ADV)
            for u in range(NU):
                turned_keys(u)
                if u > 0:
                    head_hi(u - 1, last(u - 1))
                if u + 1 < NU:
                    key_gates(u + 1)
                    decays(u + 1)
                    query_gate(u + 1)
                states(u)
                for e in range(last(u) + 1):
                    head_out(u, e)
                    out_gate(u, e)
                    head_rms(u, e)
                    if e < last(u):
                        head_hi(u, e)
            head_hi(NU - 1, last(NU - 1))
            ahead(C_O0 - 1)
            assert hp[0] == C_O0 + LEAD
            for m in range(KT):
                hi(C_O0 + m + LEAD)
                next_x(1, C_O0, m)
            rms(1)
            ffn(0)
            def take(c, dst):
                ahead(c)
                wait_done(act, c)
                act.activation(dst.rearrange("p (h t) -> p h t", h=2), pair(c), ACT.Copy).then_inc(frees(c), 1)

            def relus(n):
                m = P if n < 3 else TS
                for h in range(4):
                    act.wait_ge(sc_done, 4 * n + h + 1)
                    if n > 0:
                        act.wait_ge(sc_acc, 4 * (n - 1) + h + 1)
                    act.activation(relu[0:m, h, 0:nks[n]], ps[0:m, 4 + h, 0:nks[n]], ACT.Relu, scale=1.0 / 16.0).then_inc(sc_relu, 1)

            def out_tm(name, src):
                for pre, s, n in (("p_", src[:, 0:NT], TP), ("s_", src[0:TS, NT], TS)):
                    dst = O[pre + name][0, 0]
                    if len(dst.shape) == 3:
                        dst = dst.rearrange("t h n -> t (h n)")
                    if n == TP:
                        dst = dst.rearrange("(i p) n -> p i n", p=P)
                    act.dma_start(dst, s).then_inc(m1_out, 16)

            def take_keys(dst, n, base):
                for i in range(NT + 1):
                    m = P if i < NT else TS
                    act.wait_ge(k_turned, base + i + 1)
                    act.activation(dst[0:m, i, 0:n], ps[0:m, 4 + i % 4, 0:n], ACT.Copy).then_inc(k_taken, 1)
                act.wait_ge(k_taken, base + NT + 1)

            def attention(dsa):
                X0, PX = NX * dsa, 5 * dsa

                def exps(x):
                    act.wait_ge(at_mx, X0 + x + 1)
                    if x >= 3:
                        act.wait_ge(at_t, X0 + x - 2)
                    for j, (i, c, nk) in enumerate(groups[x][1] or [(NT, 0, KS)]):
                        ins = act.activation(prob[:, x % 3, c:c + nk], ps[:, x % 4, c:c + nk], ACT.Exp, bias=nmx[:, x % 4, j:j + 1],
                                             scale=1.0 / 8.0, accum_out=psums[:, x % 4, j:j + 1])
                    ins.then_inc(at_e, 1)

                def copies(x):
                    act.wait_ge(at_t, X0 + x + 1)
                    if x >= 2:
                        act.wait_ge(at_v, X0 + x - 1)
                    tiles = groups[x][1]
                    b = ps[:, 4 + x % 2, :]
                    if tiles is None:
                        act.activation(pt[:, x % 2, 0:2 * P], b[:, 0:2 * P], ACT.Copy)
                        act.activation(pt[0:TS, x % 2, 2 * P:3 * P], b[0:TS, 2 * P:3 * P], ACT.Copy).then_inc(at_c, 1)
                    else:
                        n = tiles[-1][1] + tiles[-1][2]
                        act.activation(pt[:, x % 2, 0:n], b[:, 0:n], ACT.Copy).then_inc(at_c, 1)

                def outputs(x):
                    pi = pairs_end.index(x)
                    act.wait_ge(at_v, X0 + x + 1)
                    b = ps[:, 6 + (PX + pi) % 2, :]
                    if pi < 4:
                        act.activation(oh[:, 4 * dsa + pi, 0:TP], b, ACT.Copy).then_inc(at_h, 1)
                    else:
                        act.activation(oh[:, 4 * dsa:4 * dsa + 4, TP:T], b[:, 0:4 * TS].rearrange("p (t n) -> p t n", t=4), ACT.Copy)\
                           .then_inc(at_h, 1)

                exps(0)
                exps(1)
                for x in range(NX + 1):
                    if x + 2 < NX:
                        exps(x + 2)
                    if x < NX:
                        copies(x)
                    if x - 1 in pairs_end:
                        outputs(x - 1)

            hp[0] = C_M1 + LEAD
            for c in range(C_M1, C_M1 + 4):
                ahead(c)
            rms(2, 2 * (jof["norm"] % 2))
            wait_done(act, C_M1 + 3)
            for i in range(NT + 1):
                m, b = (P, 4 + i) if i < NT else (TS, 2 * (jof[C_M1] % 2))
                act.activation(dv[0:m, i, :], ps[0:m, b, 0:P], ACT.Copy, scale=rcol[0:m, i:i + 1])
                act.activation(stage[0:m, i, :], ps[0:m, b, P:TBW], ACT.Copy, scale=rcol[0:m, i:i + 1]).then_inc(tb_out if i < NT else frees(C_M1), 1)
            ahead(C_CF)
            wait_freed(act, C_CF)
            ch.link(act.activation(lf_a, lf_z, ACT.Abs, bias=fb))
            ch.link(act.activation(lf_a, lf_a, ACT.Exp, scale=-1.0))
            act.activation(lf_a, lf_a, ACT.Ln, bias=ones[0:CH, 0:1]).then_inc(lf_abs, 1)
            act.wait_ge(tb_out, NT)
            act.wait_ge(frees(C_M1), jof[C_M1] // 2 + 1)
            out_tm("dsa_v", dv)
            out_tm("dsa_ik", stage[:, :, 4 * IDX:5 * IDX])
            for r, parts in enumerate([[(0, 0, P, iqT[:, 0]), (1, 0, P, iqT[:, 1])], [(0, 0, IDX, ikT), (1, IDX, P, ikT)]]):
                act.wait_ge(i_turned, r + 1)
                for n, p0, p1, dst in parts:
                    for b, n0, n1 in split:
                        act.activation(dst[p0:p1, n0:n1], ps[p0:p1, 4 + 2 * n + b, 0:n1 - n0], ACT.Copy).then_inc(i_out, 1)
            take(C_CK[0], kT[:, 0])
            act.wait_ge(lf_turned, 1)
            act.activation(lft[:, 0:NT, :], ps[:, 4, 0:NT * CH].rearrange("p (i n) -> p i n", n=CH), ACT.Copy)
            act.activation(lft[0:TS, NT, :], ps[0:TS, 4, NT * CH:(NT + 1) * CH], ACT.Copy).then_inc(lf_out, 1)
            act.wait_ge(lf_out, 1)
            out_tm("fox_logf", lft)
            relus(0)
            for n in range(3):
                take(C_CK[n + 1], kT[:, n + 1])
                relus(n + 1)
            act.wait_ge(cp_done, 1)
            take(C_CQ[0], qT[:, 0])
            take(C_CQ[1], qT[:, 1])
            for c in range(C_CV, C_CV + 4):
                ahead(c)
            wait_done(act, C_CV + 3)
            act.wait_ge(sc_acc, 16)
            for i in range(NT + 1):
                m, b = (P, 4 + i) if i < NT else (TS, 2 * (jof[C_CV] % 2))
                act.activation(cv[0:m, i, :], ps[0:m, b, :], ACT.Copy, scale=rcol[0:m, i:i + 1]).then_inc(cv_out if i < NT else frees(C_CV), 1)
            act.wait_ge(cv_out, NT)
            act.wait_ge(frees(C_CV), jof[C_CV] // 2 + 1)
            out_tm("fox_v", cv)
            take(C_CQ[2], qT[:, 2])
            take(C_CQ[3], qT[:, 3])
            act.wait_ge(m1_out, 16 * 8)
            take_keys(k_out, CH * HD, 0)
            out_tm("fox_k", k_out)
            attention(0)
            for c in [C_DK] + C_DQ:
                ahead(c)
            act.wait_ge(m1_out, 16 * 10)
            take_keys(k_out[:, :, 0:P], P, NT + 1)
            out_tm("dsa_k", k_out[:, :, 0:P])
            attention(1)
            ahead(C_O1 - 1)
            act.wait_ge(m1_out, 16 * 12)
            assert hp[0] == C_O1 + LEAD
            for m in range(KT):
                hi(C_O1 + m + LEAD)
                next_x(3, C_O1, m)
            rms(3)
            ffn(1)
            rms(4)

        @block.tensor
        def _(pe):
            PASSES = ((wh, 0), (wh, 1), (wl, 0))

            def wait_pair(j, jx=0):
                if j >= 2 or not isinstance(jx, int):
                    pe.wait_ge(pair_free[j % 2], j // 2 + jx)

            def job(c, xs, it=0, n=KT, M=P, ready=None):
                pe.wait_ge(lo_done, c + 1 + 4 * it)
                wait_pair(jof[c], 2 * it)
                s, b = c % SLOTS, 2 * (jof[c] % 2)
                for k in range(n):
                    if ready is not None:
                        ready(k)
                    for a, (w, x) in enumerate(PASSES):
                        for h in range(2):
                            mm = pe.matmul(ps[0:M, b + h, 0:HALF], w[:, s, k * M:(k + 1) * M],
                                           xs[x][:, k, h * HALF:(h + 1) * HALF],
                                           start=(k == 0 and a == 0), stop=(k == n - 1 and a == 2))
                mm.then_inc(chunk_done, 1)

            pe.wait_ge(s_const, 3)
            pe.wait_ge(s_par, 16 * len(rows))
            pe.transpose(ps[:, 7, 0:NPR], par_in[0:NPR, :], ident[0:NPR, 0:NPR]).then_inc(s_part, 1)
            pe.wait_ge(s_in, 16 * (NT + 1))
            for k in range(KT):
                wait_pair(k)
                b = 2 * (k % 2)
                for i in range(NT):
                    pe.transpose(ps[:, b, i * P:(i + 1) * P], x_in[:, i, k * P:(k + 1) * P], ident[:, :])
                pe.transpose(ps[:, b + 1, 0:TS], xs_in[:, k * P:(k + 1) * P], ident[0:TS, 0:TS]).then_inc(x_turned, 1)

            def first_norm():
                pe.wait_ge(s_part, 2)
                for k in range(KT):
                    pe.wait_ge(s_sq, k + 1)
                    for h in range(2):
                        mm = pe.matmul(ps[:, 6 + h, 0:HALF], ones[:, :], nsq[:, k % NR, h * HALF:(h + 1) * HALF],
                                       start=(k == 0), stop=(k == KT - 1))
                    mm.then_inc(s_ss, 1)

            def norm(n, b=6):
                pe.wait_ge(s_acc, (KT - 1) * n)
                if n < 4:
                    for h in range(2):
                        mm = pe.matmul(ps[:, b + h, 0:HALF], ones[:, :], acc[:, h * HALF:(h + 1) * HALF], start=True, stop=True)
                if n in (2, 4):
                    for i in range(NT + 1):
                        m = P if i < NT else TS
                        mm = pe.matmul(ps[0:m, b, HALF + i:HALF + i + 1], acc[:, i * P:i * P + m], ones[:, 0:1],
                                       start=True, stop=True)
                mm.then_inc(s_ss, 1)

            def xready(n):
                return lambda k: pe.wait_ge(s_nl, KT * n + k + 1)

            def ffn_part(l, cb, itp, hx, n, first=False):
                xr = xready(1 + 2 * l)
                if first:
                    job(cb, (xh, xl), itp, ready=xr)
                    norm(1 + 2 * l)
                    for k in range(1, 4):
                        job(cb + k, (xh, xl), itp, ready=xr)
                with pe.Fori(int(first), n // 2) as i:
                    for k in range(4):
                        job(cb + k, (xh, xl), itp + i, ready=xr)
                with pe.Fori(0, 2) as i:
                    for k in range(4):
                        job(cb + 2 * n + k, (oh, ol), itp + i, n=n, ready=lambda k: pe.wait_ge(f_lo, FT * l + hx + k + 1))

            def ffn(l):
                for part in range(2):
                    ffn_part(l, C_F[l], part * 6, part * PART, PART, part == 0)
                ffn_part(l, C_F[l] + 48, 0, 2 * PART, FT - 2 * PART)

            def out_projection(c0, ready):
                for m in range(KT):
                    job(c0 + m, (oh, ol), ready=ready)

            first_norm()
            def tm_section(c0, N, ready=None, between=None):
                wait_pair(jof[c0])
                for q in range(KT // 2):
                    pe.wait_ge(lo_done, c0 + q + 1)
                    s = (c0 + q) % SLOTS
                    for kk in range(2):
                        k = 2 * q + kk
                        if ready is not None:
                            ready(k)
                        for i in range(NT + 1):
                            out = ps[:, 4 + i, 0:N] if i < NT else ps[0:TS, 2 * (jof[c0] % 2), 0:N]
                            for a, (w, x) in enumerate(PASSES):
                                mm = pe.matmul(out, (xh, xl)[x][:, k, i * P:min(T, (i + 1) * P)], w[:, s, kk * N:(kk + 1) * N],
                                               start=(k == 0 and a == 0), stop=(k == KT - 1 and a == 2))
                    mm.then_inc(chunk_done, 1)
                    if q == 0 and between is not None:
                        between()

            def key_jobs(u):
                kind, i, hs, s0 = unit(u)
                if kind == "b":
                    j = jof["gk", u]
                    wait_pair(j)
                    wait_freed(pe, C_LR)
                    for h in range(2):
                        mm = pe.matmul(ps[:, 2 * (j % 2) + h, 0:HALF], wgk[:, i * P:(i + 1) * P],
                                       lrT[:, h * HALF:(h + 1) * HALF], start=True, stop=True)
                    mm.then_inc(gk_done, 1)
                job(c_key[u], (xh, xl))

            def at(b, n0, n1):
                k = int(n0 >= 2 * P)
                return ps[:, b + k, n0 - 2 * P * k:n1 - 2 * P * k]

            def scores(u, e, b):
                ko, kz, vc, hd = unit(u)[2][e]
                for t in range(NT + 1):
                    n0, n1 = t * P, min(T, (t + 1) * P)
                    mm = pe.matmul(at(b, n0, n1)[0:n1 - n0], kp[ko:ko + kz, u % 2, n0:n1], qp[ko:ko + kz, u % 2, n0:n1],
                                   start=True, stop=True)
                mm.then_inc(r_att, 1)

            def turn_and_score(u):
                pe.wait_ge(u_dve, UD[u + 1])
                if u > 0:
                    pe.wait_ge(r_r, (NB + 1) * u)
                for t in range(NT + 1):
                    n = P if t < NT else TS
                    b, o = (4, t * P) if t < 2 else (5, (t - 2) * P)
                    mm = pe.transpose(ps[0:n, b, o:o + P], kp[:, u % 2, t * P:t * P + n], ident[:, :])
                mm.then_inc(r_kt, 1)
                scores(u, 0, 6)
                if last(u):
                    wait_pair(jof["score", u])
                    scores(u, 1, 2 * (jof["score", u] % 2))

            def update(u, n, out):
                for ko, kz, vc, hd in unit(u)[2]:
                    q = n % 4 * BLK
                    mm = pe.matmul(out[ko:ko + kz], ktm[q:q + BLK, n // 4, ko:ko + kz], val[q:q + BLK, n // 4, vc:vc + ADV],
                                   start=True, stop=True)
                return mm

            def updates(u):
                pe.wait_ge(r_ktm, 3 * (u + 1))
                pe.wait_ge(r_attm, 3 * (u + 1))
                for q in range(4):
                    for t in range(NT):
                        mm = update(u, 4 * t + q, ps[:, 4 + q, t * P:(t + 1) * P])
                    mm.then_inc(r_w, 1)

            def outputs(u):
                kind, i, hs, s0 = unit(u)
                base = (NB + 1) * u
                pe.wait_ge(r_r, base + NB - 3)
                update(u, NB, ps[:, 4, 0:P]).then_inc(r_w, 1)
                pe.wait_ge(r_r, base + NB)
                for e, (ko, kz, vc, hd) in enumerate(hs):
                    ob = obank(e)
                    if e:
                        wait_freed(pe, ("score", u))
                        pe.wait_ge(r_r, base + NB + 1)
                    for t in range(NT + 1):
                        n0, n1 = t * P, min(T, (t + 1) * P)
                        pe.matmul(at(ob, n0, n1), val[0:n1 - n0, t, vc:vc + ADV], att[0:n1 - n0, e, n0:n1],
                                  start=True, stop=False, skip_group_check=True)
                        for n in range(4 * t, n1 // BLK):
                            if n > 0:
                                st = rst[ko:ko + kz, n - 1, :] if n < NB else s0[ko:ko + kz, :]
                                mm = pe.matmul(at(ob, n * BLK, (n + 1) * BLK), st, q2[ko:ko + kz, u % 2, n * BLK:(n + 1) * BLK],
                                               start=False, stop=True, skip_group_check=True)
                    mm.then_inc(r_o, 1)

            def squares_sum(u, e):
                j = jof["sum", u, e]
                pe.wait_ge(r_osb, heads_before[u] + e + 1)
                wait_pair(j)
                for h in range(2):
                    mm = pe.matmul(ps[:, 2 * (j % 2) + h, 0:HALF], ones[:, :], osq[:, h * HALF:(h + 1) * HALF], start=True, stop=True)
                mm.then_inc(r_oss, 1)

            X0 = (xh, xl)
            tm_section(0, AH * ADV, ready=xready(0))
            job(C_LR, X0, M=RANK)
            pe.wait_ge(s_m0in, 64)
            key_jobs(0)
            job(c_query[0], X0)
            pe.wait_ge(s_val, NT)
            tm_section(C_BV, BH * BDV)
            pe.wait_ge(s_val, 2 * NT)
            wait_freed(pe, C_BV)
            for u in range(NU):
                more, g = u + 1 < NU, list(c_gates[u])
                turn_and_score(u)
                if more:
                    key_jobs(u + 1)
                else:
                    job(g.pop(0), X0)
                updates(u)
                if more:
                    job(c_query[u + 1], X0)
                outputs(u)
                for e in range(last(u) + 1):
                    if g:
                        job(g.pop(0), X0)
                    squares_sum(u, e)
            out_projection(C_O0, lambda k: pe.wait_ge(o_lo, AH + BH))
            ffn(0)
            pe.wait_ge(s_const, 2)
            pe.wait_ge(s_m1in, 16 * 8)
            for t in range(4):
                for i in range(2):
                    mm = pe.transpose(ps[:, 4 + t // 2, (t % 2) * PAST + i * P:(t % 2) * PAST + (i + 1) * P],
                                      ck_raw[:, i, t * P:(t + 1) * P], ident[:, :])
            mm.then_inc(c_turned, 1)
            pe.wait_ge(c_out, 2)
            for i in range(2):
                pe.transpose(ps[:, 4, i * P:(i + 1) * P], dk_raw[:, i, :], ident[:, :])
                pe.transpose(ps[:, 4, PAST + i * P:PAST + (i + 1) * P], ik_raw[:, i, :], ident[:, :])
                mm = pe.transpose(ps[0:CH, 5, i * P:(i + 1) * P], lf_raw[:, i, :], ident[:, :])
            mm.then_inc(c_turned, 1)
            def turn_idx(cols4):
                for n, (c0, m) in enumerate(cols4):
                    for i in range(NT + 1):
                        b, o = 4 + 2 * n + i // 2 if i < NT else 5 + 2 * n, (i % 2) * P if i < NT else 2 * P
                        w_ = P if i < NT else TS
                        mm = pe.transpose(ps[0:m, b, o:o + w_], stage[0:w_, i, c0:c0 + m], ident[0:w_, 0:w_])
                mm.then_inc(i_turned, 1)

            def scores(n):
                if n == 0:
                    pe.wait_ge(i_out, 8)
                    pe.wait_ge(lf_out, 1)
                q0, m = ((n + 1) * P, P) if n < 3 else (TP, TS)
                for h in range(4):
                    if n > 0:
                        pe.wait_ge(sc_relu, 4 * (n - 1) + h + 1)
                    r0, a = (h % 2) * IDX, h // 2
                    q = iqT[r0:r0 + IDX, a, q0:q0 + m]
                    if n < 3:
                        mm = pe.matmul(ps[0:m, 4 + h, 0:nks[n]], q, ikT[r0:r0 + IDX, 0:nks[n]], start=True, stop=True)
                    else:
                        pe.matmul(ps[0:m, 4 + h, 0:PAST], q, ikc[r0:r0 + IDX, :], start=True, stop=True)
                        mm = pe.matmul(ps[0:m, 4 + h, PAST:KS], q, ikT[r0:r0 + IDX, TP:T], start=True, stop=True)
                    mm.then_inc(sc_done, 1)

            def attention(dsa):
                X0, PX = NX * dsa, 5 * dsa
                v, vc_ = (dv, dvc) if dsa else (cv, cvc)

                def heads_of(x):
                    h, tiles = groups[x]
                    out = []
                    for k in ([h] if tiles is not None else range(4 * h, 4 * h + 4)):
                        t, e = k // 2, k % 2
                        r = slice(e * HD, (e + 1) * HD)
                        c0 = e * HD if dsa else k * HD
                        out.append((k, t, e, kT[r, 0 if dsa else t, :], dkc[r, :] if dsa else ckc[r, t, :], slice(c0, c0 + HD), 32 * (k % 4)))
                    return out

                def masks(x):
                    h, tiles = groups[x]
                    L = ps[:, x % 4, :]
                    if x >= 4:
                        pe.wait_ge(at_e, X0 + x - 3)
                    if tiles is None:
                        for k, t, e, _, _, _, o in heads_of(x):
                            if dsa:
                                mm = pe.matmul(L[o:o + 32, 0:KS], identb[0:TS, 0:TS], mb[4][0:TS, :], start=True, stop=False,
                                               skip_group_check=True, tile_position=(0, o))
                            else:
                                pe.matmul(L[o:o + 32, 0:KS], sel[0:96, k, 0:TS], cp[0:96, TP:W], start=True, stop=False,
                                          skip_group_check=True, tile_position=(0, o))
                                mm = pe.matmul(L[o:o + 32, PAST:KS], identb[0:TS, 0:TS], caus[0:TS, 0:TS], start=False, stop=False,
                                               skip_group_check=True, tile_position=(0, o))
                    else:
                        for i, o, nk in tiles:
                            if dsa:
                                mm = pe.matmul(L[:, o:o + nk], identb[:, :], mb[i], start=(o == 0), stop=False, skip_group_check=True)
                            else:
                                pe.matmul(L[:, o:o + nk], sel[0:96, h, :], cp[0:96, 0:nk], start=(o == 0), stop=False, skip_group_check=True)
                                mm = pe.matmul(L[:, o + i * P:o + nk], identb[:, :], caus, start=False, stop=False, skip_group_check=True)
                    mm.then_inc(at_m, 1)

                def logits(x):
                    h, tiles = groups[x]
                    L = ps[:, x % 4, :]
                    pe.wait_ge(at_m, X0 + x + 1)
                    for k, t, e, ks_, kc_, _, o in heads_of(x):
                        q = qT[e * HD:(e + 1) * HD, t, :]
                        if tiles is None:
                            pe.matmul(L[o:o + 32, 0:PAST], q[:, TP:T], kc_, start=False, stop=True, skip_group_check=True,
                                      tile_position=(e * HD, o))
                            mm = pe.matmul(L[o:o + 32, PAST:KS], q[:, TP:T], ks_[:, TP:T], start=False, stop=True,
                                           skip_group_check=True, tile_position=(e * HD, o))
                        else:
                            for i, c, nk in tiles:
                                mm = pe.matmul(L[:, c:c + nk], q[:, i * P:(i + 1) * P], ks_[:, 0:nk], start=False, stop=True,
                                               skip_group_check=True)
                    mm.then_inc(at_l, 1)

                def turn(x):
                    pe.wait_ge(at_p, X0 + x + 1)
                    if x >= 2:
                        pe.wait_ge(at_c, X0 + x - 1)
                    tiles = groups[x][1]
                    n = KS if tiles is None else tiles[-1][1] + tiles[-1][2]
                    for c in range(0, n, P):
                        m = min(P, n - c)
                        mm = pe.transpose(ps[0:m, 4 + x % 2, c:c + P], prob[:, x % 3, c:c + m], ident[:, :])
                    mm.then_inc(at_t, 1)

                def values(x):
                    pi = [n for n, last in enumerate(pairs_end) if x <= last][0]
                    if pi + PX >= 2:
                        pe.wait_ge(at_o, PX + pi - 1)
                    pe.wait_ge(at_c, X0 + x + 1)
                    tiles = groups[x][1]
                    for k, t, e, _, _, vcol, o in heads_of(x):
                        out = ps[e * HD:(e + 1) * HD, 6 + (PX + pi) % 2, :]
                        if tiles is None:
                            for kb in range(3):
                                vv = v[0:TS, NT, vcol] if kb == 2 else vc_[:, kb, vcol]
                                m = TS if kb == 2 else P
                                mm = pe.matmul(out[:, t * TS:(t + 1) * TS], vv, pt[0:m, x % 2, kb * P + o:kb * P + o + TS],
                                               start=(kb == 0), stop=(kb == 2), skip_group_check=True)
                        else:
                            for i, c, nk in tiles:
                                for kb in range(i + 1):
                                    mm = pe.matmul(out[:, i * P:(i + 1) * P], v[:, kb, vcol], pt[:, x % 2, c + kb * P:c + (kb + 1) * P],
                                                   start=(kb == 0), stop=(kb == i), skip_group_check=True)
                    mm.then_inc(at_v, 1)

                for x in range(3):
                    masks(x)
                    logits(x)
                for x in range(NX + 1):
                    if x + 3 < NX:
                        masks(x + 3)
                    if x < NX:
                        turn(x)
                    if x + 3 < NX:
                        logits(x + 3)
                    if x >= 1:
                        values(x - 1)

            def turn_keys(src, base):
                for i in range(NT + 1):
                    n = P if i < NT else TS
                    if i == NT:
                        pe.wait_ge(k_taken, base + 1)
                    for t in range(len(src)):
                        mm = pe.transpose(ps[0:n, 4 + i % 4, t * P:(t + 1) * P], src[t][:, i * P:i * P + n], ident[:, :])
                    mm.then_inc(k_turned, 1)

            X1 = (xh, xl)
            pe.wait_ge(c_out, 5)


            def mixer_norm():
                wait_pair(jof["norm"])
                norm(2, 2 * (jof["norm"] % 2))

            tm_section(C_M1, TBW, ready=xready(2), between=mixer_norm)
            job(C_CF, X1, M=CH)
            pe.wait_ge(tb_out, NT)
            wait_freed(pe, C_M1)
            turn_idx([(0, P), (P, P)])
            pe.wait_ge(i_out, 4)
            turn_idx([(4 * IDX, IDX), (3 * IDX, P)])
            job(C_CK[0], X1)
            pe.wait_ge(i_out, 8)
            pe.wait_ge(lf_ready, 2)
            for i in range(NT + 1):
                n, c = (P, i * P) if i < NT else (TS, TP + PAST)
                mm = pe.transpose(ps[0:n, 4, i * CH:(i + 1) * CH], lf[:, c:c + n], ident[0:CH, 0:CH])
            mm.then_inc(lf_turned, 1)
            scores(0)
            for n in range(3):
                job(C_CK[n + 1], X1)
                scores(n + 1)
            job(C_CQ[0], X1)
            job(C_CQ[1], X1)
            pe.wait_ge(sc_relu, 16)
            tm_section(C_CV, CH * HD)
            job(C_CQ[2], X1)
            job(C_CQ[3], X1)
            pe.wait_ge(cv_out, NT)
            pe.wait_ge(k_scaled, 8)
            turn_keys([kT[:, t, :] for t in range(4)], 0)
            wait_freed(pe, C_CQ[3])
            wait_freed(pe, C_CQ[2])
            pe.wait_ge(k_taken, NT + 1)
            pe.wait_ge(cp_done, 1)
            pe.wait_ge(s_m1c, 3)
            attention(0)
            pe.wait_ge(at_e, NX)
            job(C_DK, X1)
            for t in range(4):
                job(C_DQ[t], X1)
            pe.wait_ge(at_o, 5)
            wait_freed(pe, C_DK)
            turn_keys([kT[:, 0, :]], NT + 1)
            wait_freed(pe, C_DQ[3])
            wait_freed(pe, C_DQ[2])
            pe.wait_ge(k_taken, 2 * (NT + 1))
            attention(1)
            pe.wait_ge(at_e, 2 * NX)
            out_projection(C_O1, lambda k: pe.wait_ge(at_o, 10))
            ffn(1)
            norm(4)
            for i in range(NT + 1):
                n = P if i < NT else TS
                if i == 0:
                    pe.wait_ge(x_scaled, KT)
                if i >= 2:
                    pe.wait_ge(y_ready, i - 1)
                for k in range(KT):
                    mm = pe.transpose(ps[0:n, 2 * (i % 2) + k // 4, (k % 4) * P:(k % 4 + 1) * P],
                                      x_out[:, k, i * P:i * P + n], ident[:, :])
                mm.then_inc(y_turned, 1)

        @block.vector
        def _(dve):
            ch = Chain(dve, dve_s)
            dve.wait_ge(s_part, 1)
            dve.tensor_copy(par[:, 0:NPR], ps[:, 7, 0:NPR]).then_inc(s_part, 1)
            for k in range(KT):
                dve.wait_ge(x_turned, k + 1)
                b = 2 * (k % 2)
                dve.tensor_copy(xT[:, k, 0:TP], ps[:, b, :])
                dve.tensor_copy(xT[:, k, TP:T], ps[:, b + 1, 0:TS]).then_inc(pair_free[k % 2], 1)

            def first_norm():
                def lo_part(k):
                    dve.wait_ge(s_nh, k + 1)
                    dve.tensor_tensor(xl[:, k, :], ntmp[:, k % NR, :], xh[:, k, :].bitcast(F32), ALU.subtract).then_inc(s_nl, 1)

                dve.wait_ge(s_rs, 1)
                dve.wait_ge(s_part, 2)
                for k in range(KT):
                    if k >= NR:
                        dve.wait_ge(s_nl, k - NR + 1)
                    dve.scalar_tensor_tensor(out=ntmp[:, k % NR, :], in0=xT[:, k, :], scalar=pc("mix0", k), in1=rstd[:, :],
                                             op0=ALU.mult, op1=ALU.mult).then_inc(s_nt, 1)
                    if k >= 1:
                        lo_part(k - 1)
                lo_part(KT - 1)

            def add_back(n, c0):
                def rest(m):
                    if n < 4:
                        dve.wait_ge(s_nh, KT * n + m + 1)
                        dve.scalar_tensor_tensor(out=xl[:, m, :], in0=xT[:, m, :], scalar=pc(norm_names[n], m),
                                                 in1=xh[:, m, :].bitcast(F32), op0=ALU.mult, op1=ALU.subtract).then_inc(s_nl, 1)
                    if m > 0:
                        dve.wait_ge(s_sq, KT * n + m + 1)
                        if m > 1:
                            dve.wait_ge(s_acc, (KT - 1) * (n - 1) + m - 1)
                        dve.tensor_tensor(acc, acc, sq2[:, m % 2, :], ALU.add).then_inc(s_acc, 1)

                for m in range(KT):
                    wait_done(dve, c0 + m)
                    dve.tensor_tensor(two(xT[:, m, :]), pair(c0 + m), two(xT[:, m, :]), ALU.add).then_inc(frees(c0 + m), 1)
                    if n == 4:
                        wait_freed(dve, c0 + m)
                        dve.tensor_scalar(x_out[:, m, :], xT[:, m, :], pc("final", m), None, ALU.mult).then_inc(x_scaled, 1)
                    if m > 0:
                        rest(m - 1)
                rest(KT - 1)

            def ffn_part(l, cb, itp, hx, n, last=False):
                with dve.Fori(0, n // 2) as i:
                    it = itp + i
                    for k in range(2):
                        h = FT * l + hx + 2 * i + k + 1
                        g, u = cb + 2 * k, cb + 2 * k + 1
                        fgk = fg[:, k, :]
                        dve.wait_ge(s_rs, 2 * l + 2)
                        wait_done(dve, g, it)
                        dve.tensor_tensor(two(fgk), pair(g), two(rstd[:, :]), ALU.mult).then_inc(frees(g), 1)
                        dve.wait_ge(f_sig, h)
                        dve.tensor_tensor(fgk, fgk, fsig[:, k, :], ALU.mult).then_inc(f_mul, 1)
                        dve.wait_ge(f_mul, h * 2 - 1)
                        dve.tensor_tensor(fgk, fgk, rstd[:, :], ALU.mult).then_inc(f_mul, 1)
                        wait_done(dve, u, it)
                        dve.wait_ge(f_mul, h * 2)
                        dve.tensor_tensor(two(fh[:, k, :]), two(fgk), pair(u), ALU.mult).then_inc(frees(u), 1)
                        dve.wait_ge(f_hi, h)
                        hid = bass.ds(i * 2 + k, 1)
                        dve.tensor_tensor(ol[:, hid, :], fh[:, k:k + 1, :], oh[:, hid, :].bitcast(F32), ALU.subtract)\
                           .then_inc(f_lo, 1)
                if last:
                    add_back(2 * l + 2, cb + 2 * n)
                    return
                with dve.Fori(0, 2) as i:
                    for k in range(4):
                        c = cb + 2 * n + k
                        wait_done(dve, c, itp + i)
                        xv = xT[:, bass.ds(i * 4 + k, 1), :].rearrange("p k (h t) -> p (k h) t", h=2)
                        dve.tensor_tensor(xv, pair(c), xv, ALU.add).then_inc(frees(c), 1)

            def ffn(l):
                with dve.Fori(0, 2) as part:
                    ffn_part(l, C_F[l], part * 6, part * PART, PART)
                ffn_part(l, C_F[l] + 48, 0, 2 * PART, FT - 2 * PART, last=True)

            first_norm()
            blocks = lambda ap: ap.rearrange("p (n l) -> p n l", l=BLK)
            c3 = lambda ap: ap.rearrange("p (n o) -> p n o", o=1)

            def key_gates(u):
                kind, i, hs, s0 = unit(u)
                c0, d0, a0 = c_key[u], UD[u], UA[u]
                if kind == "a":
                    wait_freed(dve, c0)
                    dve.tensor_scalar(t2, t1, oml[:, i:i + 1], lb[:, i:i + 1], ALU.mult, ALU.add).then_inc(u_dve, 1)
                    dve.wait_ge(u_dve, d0 + 1)
                    dve.tensor_scalar(t1, t2, -1.0, 1.0, ALU.mult, ALU.add).then_inc(u_dve, 1)
                else:
                    key = ("gk", u)
                    dve.wait_ge(u_act, a0 + 1)
                    dve.tensor_scalar(two(t4), pair(key), pc("bgk", i), 0.0, ALU.add, ALU.min).then_inc(frees(key), 1)
                    wait_freed(dve, key)
                    dve.tensor_tensor(t2, t4, t1, ALU.subtract).then_inc(u_dve, 1)

            def decays(u):
                kind, d0, a0, p = units[u][0], UD[u], UA[u], PRE[units[u][0]]
                dve.wait_ge(u_act, a0 + 1)
                dve.wait_ge(u_dve, d0 + p)
                dve.wait_ge(s_m0c, 2)
                dve.tensor_tensor_scan(t3, smask[:, :], t2, 0.0, ALU.mult, ALU.add).then_inc(u_dve, 1)
                dve.wait_ge(u_dve, d0 + p + 1)
                b = blocks(t3)
                mid, end = b[:, :, MID:MID + 1], b[:, :, BLK - 1:BLK]
                dve.tensor_tensor(blocks(t2), b, mid.broadcast_to([P, NB + 1, BLK]), ALU.subtract).then_inc(u_dve, 1)
                dve.tensor_tensor(c3(tail_), end, mid, ALU.subtract).then_inc(u_dve, 1)
                dve.tensor_copy(c3(ee), mid).then_inc(u_dve, 1)
                dve.wait_ge(u_dve, d0 + p + 4)
                dve.tensor_tensor(ee[:, 1:NB], ee[:, 1:NB], tail_[:, 0:NB - 1], ALU.add).then_inc(u_dve, 1)

            def keys(u):
                if u >= 2:
                    dve.wait_ge(r_o, heads_before[u - 1])
                dve.wait_ge(u_act, UA[u] + 5)
                if units[u][0] == "a":
                    dve.tensor_tensor(kp[:, u % 2, :], t1, t2, ALU.mult).then_inc(u_dve, 1)
                else:
                    wait_done(dve, c_key[u])
                    dve.tensor_tensor(two(kp[:, u % 2, :]), two(t2), pair(c_key[u]), ALU.mult).then_inc(frees(c_key[u]), 1)

            def queries(u):
                r, cq = u % 2, c_query[u]
                wait_done(dve, cq)
                if units[u][0] == "a":
                    dve.wait_ge(u_act, UA[u] + 6)
                    dve.tensor_tensor(two(qp[:, r, :]), two(t4), pair(cq), ALU.mult).then_inc(frees(cq), 1)
                    wait_freed(dve, cq)
                    dve.tensor_tensor(qp[:, r, :], qp[:, r, :], t3, ALU.mult).then_inc(q_decayed, 1)
                    dve.wait_ge(q_decayed, units[u][1] + 1)
                else:
                    dve.scalar_tensor_tensor(out=two(qp[:, r, :]), in0=pair(cq), scalar=BDK ** -0.5, in1=two(t3),
                                             op0=ALU.mult, op1=ALU.mult).then_inc(frees(cq), 1)
                    wait_freed(dve, cq)
                dve.tensor_tensor(blocks(q2[:, r, :]), blocks(qp[:, r, :]), c3(ex[r]).broadcast_to([P, NB + 1, BLK]), ALU.mult)\
                   .then_inc(u_dve, 1)

            def out_gate(u, e):
                c = c_gates[u][e]
                dve.wait_ge(gate_sig, heads_before[u] + e + 1)
                dve.tensor_tensor(two(gate[:, e, :]), two(gate[:, e, :]), pair(c), ALU.mult).then_inc(frees(c), 1)

            def mask_scores(u, e):
                dve.wait_ge(r_att, heads_before[u] + e + 1)
                pm = matt[:, :].bitcast(U32)
                tiles = lambda ap: ap.rearrange("p (i l) -> p i l", l=P)
                b0 = 2 * (jof["score", u] % 2) if e else 6
                for b in range(2):
                    dve.copy_predicated(tiles(att[:, e, 2 * b * P:2 * (b + 1) * P]),
                                        pm.rearrange("p (o l) -> p o l", o=1).broadcast_to([P, 2, P]),
                                        tiles(ps[:, b0 + b, 0:2 * P])).then_inc(att_parts if e else r_attm, 1)
                dve.copy_predicated(att[0:TS, e, TP:T], pm[0:TS, 0:TS], ps[0:TS, b0 + 1, 2 * P:2 * P + TS])\
                   .then_inc(frees(("score", u)) if e else r_attm, 1)

            def states(u):
                for n in range(NB):
                    dve.wait_ge(r_w, NW * u + min(n + 1, 4))
                    w = ps[:, 4 + n % 4, n // 4 * P:(n // 4 + 1) * P]
                    if n == 0:
                        dve.tensor_copy(rst[:, 0, :], w).then_inc(r_r, 1)
                    else:
                        dve.wait_ge(r_r, (NB + 1) * u + n)
                        dve.scalar_tensor_tensor(out=rst[:, n, :], in0=rst[:, n - 1, :], scalar=ex[u % 2][:, n:n + 1], in1=w,
                                                 op0=ALU.mult, op1=ALU.add).then_inc(r_r, 1)

            def final_states(u):
                dve.wait_ge(r_w, NW * u + 5)
                dve.scalar_tensor_tensor(out=rst[:, NB, :], in0=unit(u)[3], scalar=ex[u % 2][:, NB:NB + 1], in1=ps[:, 4, 0:P],
                                         op0=ALU.mult, op1=ALU.add).then_inc(r_r, 1)
                dve.wait_ge(r_r, (NB + 1) * (u + 1))
                for n in (NB - 1, NB):
                    dve.tensor_scalar(rst[:, n, :], rst[:, n, :], tx[:, u % 2, n:n + 1], None, ALU.mult).then_inc(state_final, 1)

            def head_norm(u, e):
                dve.wait_ge(r_ors, heads_before[u] + e + 1)
                gn = pc("ga" if units[u][0] == "a" else "gb")
                ch.link(dve.scalar_tensor_tensor(out=osb, in0=osb, scalar=gn, in1=osq, op0=ALU.mult, op1=ALU.mult))
                wait_freed(dve, c_gates[u][e])
                dve.tensor_tensor(osb, osb, gate[:, e, :], ALU.mult).then_inc(r_on, 1)

            def head_lo(u, e):
                h = heads_before[u] + e
                dve.wait_ge(o_hi, h + 1)
                hd = unit(u)[2][e][3]
                dve.tensor_tensor(ol[:, hd, :], osb, oh[:, hd, :].bitcast(F32), ALU.subtract).then_inc(o_lo, 1)

            l0, l1 = par[:, prow["lb0"]:prow["lb0"] + 4], par[:, prow["lb1"]:prow["lb1"] + 4]
            ch.link(dve.tensor_tensor(cm[:, 0:4], l0, l1, ALU.max))
            dve.tensor_tensor(cm[:, 4:8], l0, cm[:, 0:4], ALU.subtract).then_inc(s_lb, 1)
            dve.tensor_tensor(cm[:, 8:12], l1, cm[:, 0:4], ALU.subtract).then_inc(s_lb, 1)
            dve.wait_ge(s_lb, 3)
            ch.link(dve.tensor_tensor(cm[:, 12:16], cm[:, 4:8], cm[:, 8:12], ALU.add))
            ch.link(dve.reciprocal(cm[:, 16:20], cm[:, 12:16]))
            ch.link(dve.tensor_tensor(lb, cm[:, 4:8], cm[:, 16:20], ALU.mult))
            ch.link(dve.tensor_scalar(oml, lb, -1.0, 1.0, ALU.mult, ALU.add))
            dve.wait_ge(chunk_done, 4)
            ch.link(dve.memset(att, 0.0))
            key_gates(0)
            decays(0)
            keys(0)
            queries(0)
            dve.wait_ge(s_m0in, 64)
            for u in range(NU):
                mask_scores(u, 0)
                if last(u):
                    mask_scores(u, 1)
                if u > 0:
                    head_lo(u - 1, last(u - 1))
                    dve.wait_ge(m0_out, 32 * heads_before[u])
                if u + 1 < NU:
                    key_gates(u + 1)
                states(u)
                if u + 1 < NU:
                    decays(u + 1)
                    keys(u + 1)
                final_states(u)
                if u + 1 < NU:
                    queries(u + 1)
                for e in range(last(u) + 1):
                    out_gate(u, e)
                    head_norm(u, e)
                    if e < last(u):
                        head_lo(u, e)
            head_lo(NU - 1, last(NU - 1))
            add_back(1, C_O0)
            ffn(0)
            dve.wait_ge(c_turned, 1)
            for t in range(0, 4, 2):
                dve.tensor_copy(ckc[:, t:t + 2, :], ps[:, 4 + t // 2, :].rearrange("p (t k) -> p t k", t=2)).then_inc(c_out, 1)
            dve.wait_ge(c_turned, 2)
            dve.tensor_copy(dkc, ps[:, 4, 0:PAST]).then_inc(c_out, 1)
            dve.tensor_copy(ikc, ps[:, 4, PAST:2 * PAST]).then_inc(c_out, 1)
            dve.tensor_copy(lf[:, TP:TP + PAST], ps[0:CH, 5, 0:PAST]).then_inc(c_out, 1)
            def logf_and_cum():
                bz = 2 * (jof[C_CF] % 2)
                dve.wait_ge(s_rs, 3)
                wait_done(dve, C_CF)
                dve.tensor_tensor(two(lf_z), ps[0:CH, bz:bz + 2, 0:HALF], two(rstd[0:CH, :]), ALU.mult).then_inc(frees(C_CF), 1)
                dve.wait_ge(lf_abs, 1)
                ch.link(dve.tensor_scalar(lf_z, lf_z, fb, 0.0, ALU.add, ALU.min))
                dve.tensor_tensor(lf[:, 0:TP], lf_z[:, 0:TP], lf_a[:, 0:TP], ALU.subtract).then_inc(lf_ready, 1)
                dve.tensor_tensor(lf[:, TP + PAST:W], lf_z[:, TP:T], lf_a[:, TP:T], ALU.subtract).then_inc(lf_ready, 1)
                dve.wait_ge(lf_ready, 2)
                for n0, n1 in ((0, TP), (TP, W)):
                    ch.link(dve.tensor_tensor_scan(lf_cum[:, n0:n1], ones[0:CH, 0:1].broadcast_to([CH, n1 - n0]), lf[:, n0:n1], 0.0,
                                                   ALU.mult, ALU.add))
                ch.link(dve.tensor_scalar(lf_cum, lf_cum, -8.0, None, ALU.mult))
                dve.wait_ge(s_m1c, 3)
                for b in range(3):
                    part = cp[32 * b:32 * b + CH, :]
                    ins = dve.tensor_copy(part, lf_cum)
                    if b < 2:
                        ch.link(ins)
                        ch.link(dve.tensor_tensor(lf_cum, lf_cum, part, ALU.subtract))
                    else:
                        ins.then_inc(cp_done, 1)

            def add_scores(n):
                m = P if n < 3 else TS
                i = n + 1
                for h in range(4):
                    w_ = stage[0:m, i, 5 * IDX + h:5 * IDX + h + 1]
                    dve.wait_ge(sc_relu, 4 * n + h + 1)
                    r = relu[0:m, h, 0:nks[n]]
                    if h == 0:
                        dve.tensor_scalar(idx[n][0:m, :], r, w_, None, ALU.mult).then_inc(sc_acc, 1)
                    else:
                        dve.wait_ge(sc_acc, 4 * n + h)
                        dve.scalar_tensor_tensor(out=idx[n][0:m, :], in0=r, scalar=w_, in1=idx[n][0:m, :], op0=ALU.mult, op1=ALU.add)\
                           .then_inc(sc_acc, 1)

            def choose(n):
                m = P if n < 3 else TS
                s = idx[n][0:m, :]
                if n < 3:
                    ch.link(dve.memset(idx[n][0:CHUNK, nks[n] - CHUNK:nks[n]], NEG))
                for _ in range((TOPP if n < 3 else TOPS) // 8):
                    ch.link(dve.max(m8[0:m, :], s))
                    ch.link(dve.match_replace(s, m8[0:m, :], s, TAKEN))
                ch.link(dve.tensor_scalar(mb[n + 1][0:m, :], s, TAKEN / 2, NEG, ALU.is_gt, ALU.mult))

            def attention(dsa):
                X0, PX = NX * dsa, 5 * dsa

                def maxima(x):
                    dve.wait_ge(at_l, X0 + x + 1)
                    tl = groups[x][1] or [(NT, 0, KS)]
                    for j, (i, c, nk) in enumerate(tl):
                        ch.add(dve.tensor_reduce(mx[:, x % 4, j:j + 1], ps[:, x % 4, c:c + nk], AX_X, ALU.max))
                    dve.wait_ge(dve_s, ch.n)
                    dve.tensor_scalar(nmx[:, x % 4, 0:len(tl)], mx[:, x % 4, 0:len(tl)], -1.0 / 8.0, None, ALU.mult).then_inc(at_mx, 1)

                def normalise(x):
                    dve.wait_ge(at_e, X0 + x + 1)
                    tl = groups[x][1] or [(NT, 0, KS)]
                    ch.link(dve.reciprocal(rec[:, x % 4, 0:len(tl)], psums[:, x % 4, 0:len(tl)]))
                    for j, (i, c, nk) in enumerate(tl):
                        p_ = prob[:, x % 3, c:c + nk]
                        ins = dve.tensor_scalar(p_, p_, rec[:, x % 4, j:j + 1], None, ALU.mult)
                    ins.then_inc(at_p, 1)

                def outputs(x):
                    pi = pairs_end.index(x)
                    dve.wait_ge(at_h, PX + pi + 1)
                    b = ps[:, 6 + (PX + pi) % 2, :]
                    if pi < 4:
                        o, hh = ol[:, 4 * dsa + pi, 0:TP], oh[:, 4 * dsa + pi, 0:TP]
                    else:
                        o, hh = ol[:, 4 * dsa:4 * dsa + 4, TP:T], oh[:, 4 * dsa:4 * dsa + 4, TP:T]
                        b = b[:, 0:4 * TS].rearrange("p (t n) -> p t n", t=4)
                    dve.tensor_tensor(o, b, hh.bitcast(F32), ALU.subtract).then_inc(at_o, 1)

                maxima(0)
                maxima(1)
                normalise(0)
                for x in range(NX + 1):
                    if x + 2 < NX:
                        maxima(x + 2)
                    if x + 1 < NX:
                        normalise(x + 1)
                    if x - 1 in pairs_end:
                        outputs(x - 1)

            logf_and_cum()
            for n in range(4):
                add_scores(n)
            for n in range(4):
                choose(n)
            attention(0)
            for c in [C_DK] + C_DQ:
                dst = kT[:, 0, :] if c == C_DK else qT[:, c - C_DQ[0], :]
                wait_done(dve, c)
                dve.tensor_tensor(two(dst), pair(c), two(rstd[:, :]), ALU.mult).then_inc(frees(c), 1)
            attention(1)
            add_back(3, C_O1)
            ffn(1)
            dve.wait_ge(s_rt, 3)
            for i in range(NT + 1):
                n = P if i < NT else TS
                dve.wait_ge(y_turned, i + 1)
                dve.tensor_scalar(y_sb[0:n, i, :].rearrange("p (b t) -> p b t", b=2), ps[0:n, 2 * (i % 2):2 * (i % 2) + 2, :],
                                  rcol[0:n, i:i + 1], None, ALU.mult).then_inc(y_ready, 1)
    return nc


_INS = ["x_prompt", "x_sample", "state_hgrn", "state_gla", "cache_fox_k", "cache_fox_v", "cache_fox_logf",
        "cache_dsa_k", "cache_dsa_v", "cache_dsa_ik", "norm_mix", "norm_ffn", "norm_final", "ab_w_in", "ab_w_out",
        "hgrn_lb_logits", "hgrn_gnorm", "gla_w_gk", "gla_b_gk", "gla_gnorm", "cd_w_in", "cd_w_out", "fox_f_bias",
        "ffn_w_in", "ffn_w_out"]
_OUTS = ["y_prompt", "y_sample", "p_hgrn", "p_gla", "p_fox_k", "p_fox_v", "p_fox_logf", "p_dsa_k", "p_dsa_v",
         "p_dsa_ik", "s_hgrn", "s_gla", "s_fox_k", "s_fox_v", "s_fox_logf", "s_dsa_k", "s_dsa_v", "s_dsa_ik"]


def kernel(**inputs):
    import numpy as np
    import concourse.bacc as bacc
    from concourse.bass_utils import run_bass_kernel_spmd as run

    nc = bacc.Bacc("TRN2", target_bir_lowering=False, num_devices=1)
    arrays, I, O = {}, {}, {}
    for name in _INS:
        a = np.ascontiguousarray(inputs[name])
        arrays[f"in_{name}"] = a
        I[name] = nc.dram_tensor(f"in_{name}", a.shape, mybir.dt.from_np(a.dtype), kind="ExternalInput").ap()
    xp, xs = inputs["x_prompt"].shape, inputs["x_sample"].shape
    shapes = {"y_prompt": xp, "y_sample": xs, "p_hgrn": inputs["state_hgrn"].shape, "p_gla": inputs["state_gla"].shape,
              "s_hgrn": inputs["state_hgrn"].shape, "s_gla": inputs["state_gla"].shape}
    for q, t in (("p", xp[1]), ("s", xs[1])):
        for n in ("fox_k", "fox_v", "fox_logf", "dsa_k", "dsa_v", "dsa_ik"):
            c = inputs["cache_" + n].shape
            shapes[f"{q}_{n}"] = (*c[:2], t, *c[3:])
    for name in _OUTS:
        O[name] = nc.dram_tensor(f"out_{name}", tuple(shapes[name]), F32, kind="ExternalOutput").ap()
    build(nc, I, O)
    r = run(nc, [arrays], core_ids=[0])
    return tuple(r.results[0][f"out_{name}"] for name in _OUTS)
```

```python
from contextlib import ExitStack

import concourse.bass as bass
from concourse import mybir

ALU = mybir.AluOpType
ACT = mybir.ActivationFunctionType
F32 = mybir.dt.float32
F32R = mybir.dt.float32r
BF16 = mybir.dt.bfloat16
U32 = mybir.dt.uint32
AX_X = mybir.AxisListType.X

P = 128
SLOTS = 4
LEAD = 2


class Chain:

    def __init__(self, eng, sem):
        self.eng, self.sem, self.n = eng, sem, 0

    def add(self, ins):
        ins.then_inc(self.sem, 1)
        self.n = self.n + 1
        return self.n

    def link(self, ins):
        self.add(ins)
        self.eng.wait_ge(self.sem, self.n)


def build(nc, I, O):
    D = I["x_prompt"].shape[2]
    TP = I["x_prompt"].shape[1]
    TS = I["x_sample"].shape[1]
    T = TP + TS
    KT = D // P
    NT = TP // P
    HALF = T // 2
    AH, ADK, ADV = I["state_hgrn"].shape[2:]
    BH, BDK, BDV = I["state_gla"].shape[2:]
    PAST, CH, HD = I["cache_fox_k"].shape[2:]
    DKV = I["cache_dsa_k"].shape[3]
    IDX = I["cache_dsa_ik"].shape[3]
    RANK = I["gla_w_gk"].shape[1]
    FH = I["ffn_w_out"].shape[1]
    FT = FH // P
    PART = 8
    BLK = 32
    MID = BLK // 2 - 1
    NB = TP // BLK
    CHUNK = 64
    KS = PAST + TS
    TOPP = min(256, TP // 4)
    TOPS = min(256, KS // 4)
    DH = 8
    EPS = 1e-6
    NEG = -1e30
    TAKEN = -3e38
    EW = 1024
    assert T == (NB + 1) * BLK and TS == BLK and D == 1024 and ADK == ADV == BDV == P and BDK == 64
    assert FT == 22 and TOPP == P and HD == IDX == 64 and CH == 8 and DKV == 2

    w_ab = I["ab_w_in"][0].rearrange("(k p) n -> p k n", p=P)
    w_cd = I["cd_w_in"][0].rearrange("(k p) n -> p k n", p=P)
    w_abo = I["ab_w_out"][0].rearrange("(k p) n -> p k n", p=P)
    w_cdo = I["cd_w_out"][0]
    w_f1 = [I["ffn_w_in"][l].rearrange("(k p) n -> p k n", p=P) for l in range(2)]
    w_f2 = [I["ffn_w_out"][l].rearrange("(k p) n -> p k n", p=P) for l in range(2)]
    AQ, AF, AI, AG = 0, AH * ADK, 2 * AH * ADK, 3 * AH * ADK
    BQ = AG + AH * ADV
    BK, BV = BQ + BH * BDK, BQ + 2 * BH * BDK
    BG = BV + BH * BDV
    BLR = BG + BH * BDV
    CQ, CK, CV = 0, CH * HD, 2 * CH * HD
    CF = 3 * CH * HD
    DQ = CF + CH
    DK = DQ + DH * HD
    TB = DK + DKV * HD
    OFG = DKV * HD + 4 * IDX + IDX + 4
    TBW = OFG + CH

    plan = []
    whole = slice(0, P)

    def cols(w, k0, kn, c0, n):
        return [(whole, (kn, n), slice(0, kn), w[:, k0:k0 + kn, c0:c0 + n])]

    def section(w, c0, n):
        for k in range(0, KT, 2):
            plan.append(cols(w, k, 2, c0, n))

    units = [("b", t) for t in range(BH // 2)] + [("a", u) for u in range(AH)]
    NU = len(units)
    section(w_ab, AI, AH * ADV)
    C_LR = len(plan)
    plan.append(cols(w_ab, 0, KT, BLR, RANK))
    order = [("x", k) for k in range(KT)] + [0, C_LR]
    c_key, c_query, c_gates = [], [], [[] for _ in units]

    def unit_chunk(chunks, c0):
        chunks.append(len(plan))
        order.append(len(plan))
        plan.append(cols(w_ab, 0, KT, c0, P))

    def plan_key(u):
        if u < NU:
            kind, i = units[u]
            if kind == "b":
                order.append(("gk", u))
            unit_chunk(c_key, (AF if kind == "a" else BK) + i * P)

    def plan_query(u):
        if u < NU:
            kind, i = units[u]
            unit_chunk(c_query, (AQ if kind == "a" else BQ) + i * P)

    plan_key(0)
    plan_query(0)
    C_BV = len(plan)
    section(w_ab, BV, BH * BDV)
    order.append(C_BV)
    for u, (kind, i) in enumerate(units):
        if kind == "b":
            order.append(("score", u))
        plan_key(u + 1)
        plan_query(u + 1)
        for e, c0 in enumerate([AG + i * P] if kind == "a" else [BG + 2 * i * P, BG + (2 * i + 1) * P]):
            unit_chunk(c_gates[u], c0)
            order.append(("turn", u, e))
    C_O0 = len(plan)
    for m in range(KT):
        plan.append(cols(w_abo, 0, KT, m * P, P))
    C_F = [len(plan), 0]

    def ffn_chunks(l):
        for r in range(0, FT, PART):
            n = min(PART, FT - r)
            for j in range(r, r + n):
                plan.append(cols(w_f1[l], 0, KT, j * P, P))
                plan.append(cols(w_f1[l], 0, KT, FH + j * P, P))
            for m in range(KT):
                plan.append(cols(w_f2[l], r, n, m * P, P))

    ffn_chunks(0)
    C_M1 = len(plan)
    for k in range(0, KT, 2):
        plan.append([(whole, (2, TBW), (slice(0, 2), slice(0, OFG)), w_cd[:, k:k + 2, TB:TB + OFG]),
                     (whole, (2, TBW), (slice(0, 2), slice(OFG, TBW)), w_cd[:, k:k + 2, CF:CF + CH])])
    C_CK = [len(plan) + t for t in range(4)]
    for t in range(4):
        plan.append(cols(w_cd, 0, KT, CK + t * P, P))
    C_CQ = []
    for t in range(4):
        if t == 2:
            C_CV = len(plan)
            section(w_cd, CV, CH * HD)
        C_CQ.append(len(plan))
        plan.append(cols(w_cd, 0, KT, CQ + t * P, P))
    C_DK = len(plan)
    plan.append(cols(w_cd, 0, KT, DK, DKV * HD))
    C_DQ = [C_DK + 1 + t for t in range(4)]
    for t in range(4):
        plan.append([(whole, (KT, P), (slice(0, KT), slice(g * HD, g * HD + HD)),
                      w_cd[:, :, DQ + (4 * g + t) * HD:DQ + (4 * g + t + 1) * HD]) for g in range(2)])
    C_O1 = len(plan)
    for m in range(KT):
        ch = [(whole, (KT, P), slice(0, 4), w_cdo[0:4 * P, m * P:(m + 1) * P].rearrange("(k p) n -> p k n", p=P))]
        for g in range(2):
            r0 = 4 * P + g * 4 * HD
            ch.append((slice(g * HD, g * HD + HD), (KT, P), slice(4, 8),
                       w_cdo[r0:r0 + 4 * HD, m * P:(m + 1) * P].rearrange("(k p) n -> p k n", p=HD)))
        plan.append(ch)
    C_F[1] = len(plan)
    ffn_chunks(1)
    C_END = len(plan)
    landed = []
    use = [0] * SLOTS
    for c, ch in enumerate(plan):
        use[c % SLOTS] += 16 * len(ch)
        landed.append(use[c % SLOTS])

    order += [c for c in range(C_O0, C_END) if not (C_M1 < c < C_M1 + 4 or C_CV < c < C_CV + 4)]
    order.insert(order.index(C_M1) + 1, "norm")
    jof = {key: j for j, key in enumerate(order)}
    for c0 in (0, C_BV, C_M1, C_CV):
        for c in range(c0 + 1, c0 + 4):
            jof[c] = jof[c0]

    with ExitStack() as ctx:
        def sb(name, shape, dt=F32):
            return ctx.enter_context(nc.sbuf_tensor(name, shape, dt))

        sems = {}

        def sem(name):
            if name not in sems:
                sems[name] = ctx.enter_context(nc.semaphore(name))
            return sems[name]

        xT = sb("xT", [P, KT, T])
        xh, xl = sb("x_hi", [P, KT, T], F32R), sb("x_lo", [P, KT, T], F32R)
        oh, ol = sb("o_hi", [P, KT, T], F32R), sb("o_lo", [P, KT, T], F32R)
        raw = sb("w_raw", [P, SLOTS, EW])
        wh, wl = sb("w_hi", [P, SLOTS, EW], F32R), sb("w_lo", [P, SLOTS, EW], F32R)
        ident = sb("ident", [P, P])
        identb = sb("identb", [P, P], BF16)
        ones = sb("ones", [P, P])
        par = sb("par", [P, 64])
        small = sb("small", [P, 128])
        AR = 17408
        arena = sb("arena", [P, AR])
        ps = ctx.enter_context(nc.psum_tensor("ps", [P, 8, 512], F32))
        used = [0]

        def area(n):
            used[0] += n
            assert used[0] <= AR, used[0]
            return arena[:, used[0] - n:used[0]]

        raw_landed = [sem(f"raw_landed{s}") for s in range(SLOTS)]
        hi_done, lo_done, chunk_done = sem("hi_done"), sem("lo_done"), sem("chunk_done")
        job_done = sem("job_done")
        pair_free = [sem("pair_free0"), sem("pair_free1")]
        dve_s, act_s, pe_s, pool_s = sem("dve_s"), sem("act_s"), sem("pe_s"), sem("pool_s")
        s_in, s_par, s_const = sem("s_in"), sem("s_par"), sem("s_const")
        s_part = sem("s_part")
        s_sq, s_ss, s_rs, s_nt, s_nh, s_nl = (sem(n) for n in ("sq_done", "ss_done", "rstd_done", "norm_done", "norm_hi", "norm_lo"))
        f_sig, f_mul, f_hi, f_lo = sem("f_sig"), sem("f_mul"), sem("f_hi"), sem("f_lo")
        s_acc, s_rt, x_scaled, k_scaled = sem("squares_added"), sem("rcol_done"), sem("x_scaled"), sem("k_scaled")
        o_hi, o_lo = sem("o_hi"), sem("o_lo")
        x_turned, y_turned, y_ready = sem("x_turned"), sem("y_turned"), sem("y_ready")
        s_out = sem("s_out")

        rows, prow = [], {}
        for name, src, n in [("mix0", I["norm_mix"][0], 8), ("mix1", I["norm_mix"][1], 8), ("ffn0", I["norm_ffn"][0], 8),
                             ("ffn1", I["norm_ffn"][1], 8), ("final", I["norm_final"], 8),
                             ("lb0", I["hgrn_lb_logits"][0], 4), ("lb1", I["hgrn_lb_logits"][1], 4),
                             ("ga", I["hgrn_gnorm"][0], 1), ("gb", I["gla_gnorm"][0], 1), ("bgk", I["gla_b_gk"][0], 2)]:
            prow[name] = sum(r[1] for r in rows)
            rows.append((src.rearrange("(k p) -> k p", p=P), n))
        NPR = sum(r[1] for r in rows)

        def pc(name, k=0):
            return par[:, prow[name] + k:prow[name] + k + 1]

        eps_c = small[:, 0:1]
        norm_names = ["mix0", "ffn0", "mix1", "ffn1", "final"]

        x_in = arena[:, 0:NT * D].rearrange("p (i d) -> p i d", i=NT)
        xs_in = arena[0:TS, NT * D:(NT + 1) * D]
        par_in = arena[0:NPR, 6000:6000 + P]
        NR = 4
        nsq = arena[:, AR - NR * T:AR].rearrange("p (r t) -> p r t", r=NR)
        ntmp = nsq
        acc, sq2 = nsq[:, NR - 1, :], nsq[:, 1:NR - 1, :]
        rstd = sb("rstd", [P, T])[:, :]
        rcol = small[:, 44:44 + NT + 1]
        x_out = arena[:, 6000:6000 + KT * T].rearrange("p (k t) -> p k t", k=KT)
        y_sb = arena[:, 0:(NT + 1) * D].rearrange("p (i d) -> p i d", i=NT + 1)
        fsig = arena[:, 0:2 * T].rearrange("p (r t) -> p r t", r=2)
        fh = arena[:, 2 * T:4 * T].rearrange("p (r t) -> p r t", r=2)
        fg = arena[:, 4 * T:6 * T].rearrange("p (r t) -> p r t", r=2)

        def pair(c):
            b = 2 * (jof[c] % 2)
            return ps[:, b:b + 2, 0:HALF]

        def wait_done(eng, c, it=0):
            eng.wait_ge(chunk_done, c + 1 + 4 * it)

        def frees(c):
            return pair_free[jof[c] % 2]

        def wait_freed(eng, c, it=0):
            eng.wait_ge(frees(c), jof[c] // 2 + 1 + 2 * it)

        token_tiles = ((P, 0, NT), (TS, NT, NT + 1))

        def two(ap):
            return ap.rearrange("p (h t) -> p h t", h=2)


        used[0] = 0
        val = area((NT + 1) * D).rearrange("p (i d) -> p i d", i=NT + 1)
        qp = area(2 * T).rearrange("p (r t) -> p r t", r=2)
        kp = area(2 * T).rearrange("p (r t) -> p r t", r=2)
        q2 = area(2 * T).rearrange("p (r t) -> p r t", r=2)
        s0h = area(AH * ADV).rearrange("p (h v) -> p h v", h=AH)
        s0g = area(BH // 2 * BDV).rearrange("p (h v) -> p h v", h=BH // 2)
        att = area(2 * T).rearrange("p (r t) -> p r t", r=2)
        gate = area(2 * T).rearrange("p (r t) -> p r t", r=2)
        ktm = area((NT + 1) * P).rearrange("p (i k) -> p i k", i=NT + 1)
        rst = area((NB + 1) * ADV).rearrange("p (n v) -> p n v", n=NB + 1)
        t1, t2, t3, t4 = (area(T) for _ in range(4))
        osb, osq = area(T), area(T)
        lrT = rstd[0:RANK, :]
        m0_only = sb("m0_only", [P, BH * BDK + P + T // 2])[:, :]
        wgk = m0_only[0:RANK, 0:BH * BDK]
        matt = m0_only[:, BH * BDK:BH * BDK + P]
        smask = m0_only[:, BH * BDK + P:BH * BDK + P + T // 2].bitcast(BF16)
        cm = small[:, 1:25]
        lb, oml = small[:, 25:29], small[:, 29:33]
        tail_, ee = small[:, 33:33 + NB + 1], small[:, 50:50 + NB + 1]
        ex = [small[:, 67 + 17 * r:84 + 17 * r] for r in range(2)]
        tx = sb("tx", [P, 2, NB + 1])
        s_m0in, s_m0c, gk_done, u_act, u_dve = (sem(n) for n in ("m0_in", "m0_const", "gk_done", "unit_act", "unit_dve"))
        s_val, s_lb, gate_sig, q_decayed, state_final, att_parts = (sem(n) for n in (
            "val_done", "lb_done", "gate_sig", "q_decayed", "state_final", "att_parts"))
        r_kt, r_ktm, r_att, r_attm, r_w, r_r, r_intra, r_o, r_ors, r_tm, r_ot, m0_out = (sem(n) for n in (
            "keys_turned", "keys_copied", "att_done", "att_masked", "update_done", "state_done", "intra_done", "o_done",
            "o_rstd", "o_normed", "o_turned", "m0_out"))
        rss = [small[:, 101 + 5 * e:106 + 5 * e] for e in range(2)]

        def unit(u):
            kind, i = units[u]
            if kind == "a":
                return kind, i, [(0, P, i * ADV, i)], s0h[:, i, :]
            return kind, i, [(e * BDK, BDK, (AH + 2 * i + e) * ADV, AH + 2 * i + e) for e in range(2)], s0g[:, i, :]

        heads_before, UD, UA = ([sum(n[kind] for kind, _ in units[:u]) for u in range(NU + 1)]
                                for n in ({"a": 1, "b": 2}, {"a": 9, "b": 7}, {"a": 6, "b": 5}))
        PRE = {"a": 2, "b": 1}
        split = [(0, 0, 2 * P), (1, 2 * P, T)]

        NW = 5

        def obank(e):
            return 6 - 2 * e

        def last(u):
            return len(c_gates[u]) - 1

        used[0] = 0
        by_tile = lambda ap, k: ap.rearrange("p (k t) -> p k t", k=k)
        q_area = area(4 * T)
        qT = by_tile(q_area, 4)
        W = TP + KS
        lf, lf_cum = q_area[0:CH, 0:W], q_area[0:CH, W:2 * W]
        pt_at = used[0]
        nks = [2 * P, 3 * P, 4 * P, KS]
        idx = [area(n) for n in nks]
        pt = [arena[:, pt_at:pt_at + 512], m0_only[:, 0:512]]
        kT = by_tile(area(4 * T), 4)
        v_area = area((NT + 1) * CH * HD)
        cv = v_area.rearrange("p (i n) -> p i n", i=NT + 1)
        ck_raw = v_area[:, 0:1024].rearrange("p (i n) -> p i n", i=2)
        dk_raw = v_area[:, 1024:1280].rearrange("p (i n) -> p i n", i=2)
        ik_raw = v_area[:, 1280:1536].rearrange("p (i n) -> p i n", i=2)
        lf_raw = v_area[:, 1536:1552].rearrange("p (i n) -> p i n", i=2)
        relu = v_area[:, 0:2048].rearrange("p (h k) -> p h k", h=4)
        ckc = area(4 * PAST).rearrange("p (t k) -> p t k", t=4)
        cvc = area(2 * CH * HD).rearrange("p (i n) -> p i n", i=2)
        dv = area((NT + 1) * P).rearrange("p (i n) -> p i n", i=NT + 1)
        dkc = area(PAST)
        dvc = area(2 * P).rearrange("p (i n) -> p i n", i=2)
        mb_all = area(784).bitcast(BF16)
        mb_off = [0, P, 3 * P, 6 * P, 10 * P]
        mb = [mb_all[:, o:o + n] for o, n in zip(mb_off, [P] + nks)]
        caus = area(P // 2).bitcast(BF16)
        sel = area(CH * P // 2).bitcast(BF16).rearrange("p (h m) -> p h m", h=CH)
        cp = area(W // 2).bitcast(BF16)
        x_area = area(4096)
        ikc = x_area[:, 0:PAST]
        iqT = by_tile(x_area[:, PAST:PAST + 2 * T], 2)
        ikT = x_area[:, PAST + 2 * T:PAST + 3 * T]
        SW = TBW - DKV * HD
        stage = x_area[:, PAST + 3 * T:PAST + 3 * T + (NT + 1) * SW].rearrange("p (i n) -> p i n", i=NT + 1)
        at = PAST + 3 * T + (NT + 1) * SW
        lft, lf_z, lf_a = (x_area[:, at + n * (NT + 1) * CH:at + (n + 1) * (NT + 1) * CH].rearrange("p (i n) -> p i n", i=NT + 1)
                           for n in range(3))
        prob = x_area[:, 0:1536].rearrange("p (r k) -> p r k", r=3)
        k_out = x_area[:, 1536:4096].rearrange("p (i n) -> p i n", i=NT + 1)
        m8 = [m0_only[:, 512 + 8 * n:520 + 8 * n] for n in range(4)]
        mx, nmx, psums, rec = (small[:, 9 + 8 * n:17 + 8 * n].rearrange("p (r j) -> p r j", j=2) for n in range(4))
        fb = small[:, 49:49 + CH]
        s_m1in, s_m1c, c_turned, c_out, m1_out = (sem(n) for n in ("m1_in", "m1_const", "cache_turned", "cache_taken", "m1_out"))
        tb_out, i_turned, i_out, lf_biased, lf_abs, lf_ready, lf_turned, lf_out, cp_done = (sem(n) for n in (
            "tb_taken", "idx_turned", "idx_taken", "lf_biased", "lf_abs", "lf_ready", "lf_turned", "lf_taken", "cp_done"))
        sc_done, sc_relu, sc_acc, cv_out, k_turned, k_taken = (sem(n) for n in (
            "score_done", "score_relu", "score_added", "cv_taken", "k_turned", "k_taken"))
        at_m, at_l, at_mx, at_e, at_p, at_t, at_c, at_v, at_h, at_o = (sem(n) for n in (
            "att_masks", "att_logits", "att_max", "att_exp", "att_probs", "att_turned", "att_copied", "att_values",
            "att_hi", "att_lo"))
        N_M0_OUT = sum(2 * (1 if kind == "a" else 2) for kind, _ in units)

        groups = [(2 * t + e, tiles) for t in range(4) for e in range(2)
                  for tiles in ([(0, 0, P), (1, P, 2 * P)], [(2, 0, 3 * P)], [(3, 0, 4 * P)])]
        groups += [(w, None) for w in range(2)]
        NX = len(groups)
        pairs_end = [6 * (t + 1) - 1 for t in range(4)] + [NX - 1]
        block = ctx.enter_context(nc.Block())

        @block.sync
        def _(sp):
            def load(c, it=0, at=None):
                if c >= SLOTS or not isinstance(it, int):
                    sp.wait_ge(lo_done, c - SLOTS + 1 + 4 * it)
                for parts, shape, sub, src in plan[c]:
                    v = raw[parts, c % SLOTS, 0:shape[0] * shape[1]].rearrange("p (k n) -> p k n", k=shape[0])
                    v = v[:, sub, :] if isinstance(sub, slice) else v[:, sub[0], sub[1]]
                    sp.dma_start(v, src if at is None else at).then_inc(raw_landed[c % SLOTS], 16)

            def ffn_part(l, cb, itp, r0, n):
                with sp.Fori(0, n // 2) as i:
                    for k in range(4):
                        load(cb + k, itp + i, w_f1[l][:, :, bass.ds((i * 2 + k // 2 + r0) * P + (k % 2) * FH, P)])
                with sp.Fori(0, 2) as i:
                    for k in range(4):
                        load(cb + 2 * n + k, itp + i, w_f2[l][:, bass.ds(r0, n), bass.ds((i * 4 + k) * P, P)])

            def ffn(l):
                with sp.Fori(0, 2) as part:
                    ffn_part(l, C_F[l], part * 6, part * PART, PART)
                ffn_part(l, C_F[l] + 48, 0, 2 * PART, FT - 2 * PART)

            for i in range(NT):
                sp.dma_start(x_in[:, i, :], I["x_prompt"][0, i * P:(i + 1) * P, :]).then_inc(s_in, 16)
            sp.dma_start(xs_in, I["x_sample"][0]).then_inc(s_in, 16)
            for c in range(LEAD):
                load(c)
            off = 0
            for src, n in rows:
                sp.dma_start(par_in[off:off + n, :], src).then_inc(s_par, 16)
                off += n
            for c in range(LEAD, SLOTS):
                load(c)
            sp.dma_start(s0h, I["state_hgrn"][0, 0].rearrange("h k v -> k h v")).then_inc(s_m0in, 16)
            for e in range(2):
                sp.dma_start(s0g[e * BDK:(e + 1) * BDK], I["state_gla"][0, 0].rearrange("(i e) k v -> e k i v", e=2)[e]).then_inc(s_m0in, 16)
            sp.dma_start(wgk[:, :], I["gla_w_gk"][0]).then_inc(s_m0in, 16)
            for c in range(SLOTS, C_F[0]):
                load(c)
            sp.wait_ge(m0_out, 16 * N_M0_OUT)
            for dst, name in ((ck_raw, "fox_k"), (cvc, "fox_v"), (dk_raw, "dsa_k"), (dvc, "dsa_v")):
                sp.dma_start(dst, I["cache_" + name][0, 0].rearrange("(i p) h n -> p i (h n)", p=P)).then_inc(s_m1in, 16)
            for e in range(2):
                sp.dma_start(ik_raw[:, :, e * IDX:(e + 1) * IDX], I["cache_dsa_ik"][0, 0].rearrange("(i p) n -> p i n", p=P)).then_inc(s_m1in, 16)
            sp.dma_start(lf_raw, I["cache_fox_logf"][0, 0].rearrange("(i p) n -> p i n", p=P)).then_inc(s_m1in, 16)
            sp.dma_start(fb, I["fox_f_bias"][0:1, :].broadcast_to([P, CH])).then_inc(s_m1in, 16)
            ffn(0)
            for c in range(C_M1, C_F[1]):
                load(c)
            ffn(1)
            for i in range(NT + 1):
                sp.wait_ge(y_ready, i + 1)
                dst = O["y_prompt"][0, i * P:(i + 1) * P, :] if i < NT else O["y_sample"][0]
                sp.dma_start(dst, y_sb[0:P if i < NT else TS, i, :]).then_inc(s_out, 16)
            sp.wait_ge(s_out, 16 * (NT + 1))
            sp.wait_ge(m0_out, 16 * N_M0_OUT)
            sp.wait_ge(m1_out, 16 * 12)

        @block.gpsimd
        def _(pool):
            ch = Chain(pool, pool_s)
            ch.add(pool.memset(ident[:, :], 0.0))
            ch.add(pool.memset(identb[:, :], 0.0))
            ch.add(pool.memset(small[:, :], 0.0))
            ch.link(pool.memset(ones[:, :], 1.0))
            for t in (ident, identb):
                pool.affine_select(out=t[:, :], in_=t[:, :], compare_op=ALU.not_equal, fill=1.0, base=0,
                                   pattern=[[-1, P]], channel_multiplier=1).then_inc(s_const, 1)
            pool.memset(eps_c, EPS).then_inc(s_const, 1)

            def lo(c, it=0):
                pool.wait_ge(hi_done, c + 1 + 4 * it)
                s = c % SLOTS
                pool.tensor_tensor(wl[:, s, :], raw[:, s, :], wh[:, s, :].bitcast(F32), ALU.subtract).then_inc(lo_done, 1)

            def los(c0, c1):
                with pool.Fori(0, (c1 - c0) // 4) as i:
                    for k in range(4):
                        lo(c0 + k, i)
                for c in range(c0 + (c1 - c0) // 4 * 4, c1):
                    lo(c)

            ch.add(pool.memset(smask[:, :], 1.0))
            ch.link(pool.memset(matt[:, :], 1.0))
            pool.memset(smask[:, 0:T:BLK], 0.0).then_inc(s_m0c, 1)
            ch.link(pool.affine_select(out=matt[:, :], in_=matt[:, :], compare_op=ALU.is_ge, fill=0.0, base=0,
                                       pattern=[[1, P]], channel_multiplier=-1))
            mv = matt[:, :].rearrange("p (b l) -> p b l", l=BLK)
            pool.affine_select(out=mv, in_=mv, compare_op=ALU.is_ge, fill=0.0, base=0,
                               pattern=[[-BLK, P // BLK], [0, BLK]], channel_multiplier=1).then_inc(s_m0c, 1)
            los(0, C_F[0] + PART)
            pool.wait_ge(m0_out, 16 * N_M0_OUT)
            ch.add(pool.memset(cp[0:96, :], 0.0))
            ch.add(pool.memset(sel[0:96], 0.0))
            ch.add(pool.memset(caus, 0.0))
            ch.link(pool.memset(mb[0], 0.0))
            pool.affine_select(out=caus, in_=caus, compare_op=ALU.is_ge, fill=NEG, base=0, pattern=[[-1, P]], channel_multiplier=1)\
                .then_inc(s_m1c, 1)
            pool.memset(mb[0][0:CHUNK, CHUNK:P], NEG).then_inc(s_m1c, 1)
            for b in range(3):
                ins = pool.affine_select(out=sel[0:96], in_=sel[0:96], compare_op=ALU.not_equal, fill=1.0, base=-32 * b,
                                         pattern=[[-1, CH], [0, P]], channel_multiplier=1)
                if b < 2:
                    ch.link(ins)
                else:
                    ins.then_inc(s_m1c, 1)
            los(C_F[0] + PART, C_M1)
            for c in range(C_M1, C_O1):
                lo(c)
                if c - LEAD in C_CK + C_CQ:
                    k = c - LEAD
                    tile = kT[:, C_CK.index(k), :] if k in C_CK else qT[:, C_CQ.index(k), :]
                    wait_freed(pool, k)
                    pool.tensor_tensor(tile, tile, rstd[:, :], ALU.mult).then_inc(k_scaled, 1)
            los(C_O1, C_END)

        @block.scalar
        def _(act):
            ch = Chain(act, act_s)

            def hi(c, it=0):
                if isinstance(it, int) and c >= C_END:
                    return
                s = c % SLOTS
                act.wait_ge(raw_landed[s], landed[c] + 16 * it)
                if c >= SLOTS:
                    wait_done(act, c - SLOTS, it)
                act.activation(wh[:, s, :], raw[:, s, :], ACT.Copy).then_inc(hi_done, 1)

            def first_norm():
                for k in range(KT):
                    act.wait_ge(pair_free[k % 2], k // 2 + 1)
                    if k >= 3:
                        act.wait_ge(s_acc, k - 2)
                    act.activation(acc if k == 0 else sq2[:, k % 2, :], xT[:, k, :], ACT.Square).then_inc(s_sq, 1)
                rms(0)
                for k in range(KT):
                    act.wait_ge(s_nt, k + 1)
                    act.activation(xh[:, k, :], ntmp[:, k % NR, :], ACT.Copy).then_inc(s_nh, 1)

            def rms(n, b=6):
                act.wait_ge(s_ss, n + 1)
                act.wait_ge(s_const, 3)
                if n < 4:
                    ch.link(act.activation(two(rstd), ps[:, b:b + 2, 0:HALF], ACT.Ln, bias=eps_c, scale=1.0 / D))
                    act.activation(rstd, rstd, ACT.Exp, scale=-0.5).then_inc(s_rs, 1)
                if n in (2, 4):
                    for m, i0, i1 in token_tiles:
                        ins = act.activation(rcol[0:m, i0:i1], ps[0:m, b, HALF + i0:HALF + i1], ACT.Ln if n == 2 else ACT.Sqrt,
                                             bias=eps_c[0:m], scale=1.0 / D)
                    ins.then_inc(frees("norm") if n == 2 else s_rt, 1)
                    if n == 4:
                        return
                    wait_freed(act, "norm")
                    for m, i0, i1 in token_tiles:
                        ins = act.activation(rcol[0:m, i0:i1], rcol[0:m, i0:i1], ACT.Exp, scale=-0.5)
                    ins.then_inc(s_rt, 1)
                    act.wait_ge(s_rt, 1)

            def next_x(n, c0, m):
                wait_freed(act, c0 + m)
                if n < 4:
                    act.activation(xh[:, m, :], xT[:, m, :], ACT.Copy, scale=pc(norm_names[n], m)).then_inc(s_nh, 1)
                if m >= 3:
                    act.wait_ge(s_acc, (KT - 1) * n + m - 2)
                act.activation(acc if m == 0 else sq2[:, m % 2, :], xT[:, m, :], ACT.Square).then_inc(s_sq, 1)

            def ffn_part(l, cb, itp, hx, n, last=False):
                with act.Fori(0, n // 2) as i:
                    it = itp + i
                    for k in range(4):
                        hi(cb + k + LEAD, it)
                        if k % 2 == 0:
                            wait_freed(act, cb + k, it)
                            act.activation(fsig[:, k // 2, :], fg[:, k // 2, :], ACT.Sigmoid).then_inc(f_sig, 1)
                        else:
                            wait_freed(act, cb + k, it)
                            act.activation(oh[:, bass.ds(i * 2 + k // 2, 1), :], fh[:, k // 2:k // 2 + 1, :],
                                           ACT.Copy).then_inc(f_hi, 1)
                if last:
                    for k in range(KT):
                        hi(cb + 2 * n + k + LEAD)
                        next_x(2 * l + 2, cb + 2 * n, k)
                else:
                    with act.Fori(0, 2) as i:
                        for k in range(4):
                            hi(cb + 2 * n + k + LEAD, itp + i)

            def ffn(l):
                with act.Fori(0, 2) as part:
                    ffn_part(l, C_F[l], part * 6, part * PART, PART)
                ffn_part(l, C_F[l] + 48, 0, 0, FT - 2 * PART, last=True)

            for c in range(LEAD):
                hi(c)
            first_norm()
            hp = [LEAD]

            def ahead(c):
                while hp[0] <= c + LEAD:
                    hi(hp[0])
                    hp[0] += 1

            def key_gates(u):
                kind, i, hs, s0 = unit(u)
                c0, d0 = c_key[u], UD[u]
                ahead(c0)
                act.wait_ge(u_dve, d0)
                if kind == "a":
                    wait_done(act, c0)
                    act.activation(two(t1), pair(c0), ACT.Sigmoid).then_inc(frees(c0), 1)
                    act.wait_ge(u_dve, d0 + 2)
                    act.activation(t2, t2, ACT.Ln).then_inc(u_act, 1)
                else:
                    act.wait_ge(gk_done, i + 1)
                    ch.link(act.activation(two(t1), pair(("gk", u)), ACT.Abs, bias=pc("bgk", i)))
                    ch.link(act.activation(t1, t1, ACT.Exp, scale=-1.0))
                    act.activation(t1, t1, ACT.Ln, bias=ones[:, 0:1]).then_inc(u_act, 1)

            def decays(u):
                kind, a0, d0 = units[u][0], UA[u], UD[u]
                scale = 1.0 if kind == "a" else 1.0 / 16.0
                act.wait_ge(u_dve, d0 + PRE[kind] + 5)
                act.activation(ex[u % 2], ee, ACT.Exp, scale=scale).then_inc(u_act, 1)
                act.activation(tx[:, u % 2, :], tail_, ACT.Exp, scale=scale).then_inc(u_act, 1)
                act.activation(t3, t2, ACT.Exp, scale=scale).then_inc(u_act, 1)
                act.wait_ge(u_act, a0 + (5 if kind == "a" else 4))
                act.activation(t2, t2, ACT.Exp, scale=-scale).then_inc(u_act, 1)

            def query_gate(u):
                ahead(c_query[u])
                if units[u][0] == "a":
                    wait_done(act, c_query[u])
                    act.activation(two(t4), pair(c_query[u]), ACT.Sigmoid).then_inc(u_act, 1)

            def out_gate(u, e):
                c = c_gates[u][e]
                ahead(c)
                act.wait_ge(o_lo, heads_before[u])
                wait_done(act, c)
                act.activation(two(gate[:, e, :]), pair(c), ACT.Sigmoid).then_inc(gate_sig, 1)

            def turned_keys(u):
                act.wait_ge(r_kt, u + 1)
                if u > 0:
                    act.wait_ge(r_w, NW * u)
                for b in range(2):
                    act.activation(ktm[:, 2 * b:2 * b + 2, :], ps[:, 4 + b, 0:2 * P].rearrange("p (i k) -> p i k", k=P), ACT.Copy)\
                       .then_inc(r_ktm, 1)
                act.activation(ktm[0:TS, NT, :], ps[0:TS, 5, 2 * P:3 * P], ACT.Copy).then_inc(r_ktm, 1)

            def states(u):
                kind, i, hs, s0 = unit(u)
                act.wait_ge(state_final, 2 * (u + 1))
                for ko, kz, vc, hd in hs:
                    for out, n in (("p_", NB - 1), ("s_", NB)):
                        dst = O[out + "hgrn"][0, 0, hd] if kind == "a" else O[out + "gla"][0, 0, hd - AH]
                        act.dma_start(dst, rst[ko:ko + kz, n, :]).then_inc(m0_out, 16)

            def head_out(u, e):
                h = heads_before[u] + e
                act.wait_ge(r_o, h + 1)
                if h > 0:
                    act.wait_ge(r_ors, h)
                ob = obank(e)
                for t in range(NT):
                    ins = act.activation(osq[:, t * P:(t + 1) * P], ps[:, ob, t * P:(t + 1) * P], ACT.Square, accum_out=rss[e][:, t:t + 1])
                ch.link(ins)
                ch.link(act.activation(osq[0:TS, 0:P], ps[0:TS, ob + 1, 0:P], ACT.Square, accum_out=rss[e][0:TS, NT:NT + 1]))
                for m, i0, i1 in token_tiles:
                    r = rss[e][0:m, i0:i1]
                    ins = act.activation(r, r, ACT.Sqrt, bias=eps_c[0:m], scale=1.0 / ADV)
                ins.then_inc(r_ors, 1)

            def head_hi(u, e):
                h = heads_before[u] + e
                wait_freed(act, ("turn", u, e))
                act.activation(oh[:, unit(u)[2][e][3], :], osb, ACT.Copy).then_inc(o_hi, 1)

            def take_values(c0, v0):
                for c in range(c0, c0 + 4):
                    ahead(c)
                wait_done(act, c0 + 3)
                for i in range(NT):
                    act.activation(val[:, i, v0:v0 + 512], ps[:, 4 + i, :], ACT.Copy).then_inc(s_val, 1)
                act.activation(val[0:TS, NT, v0:v0 + 512], ps[0:TS, 2 * (jof[c0] % 2), :], ACT.Copy).then_inc(frees(c0), 1)

            act.wait_ge(s_lb, 2)
            act.activation(cm[:, 4:12], cm[:, 4:12], ACT.Exp).then_inc(s_lb, 1)
            take_values(0, 0)
            ahead(C_LR)
            wait_done(act, C_LR)
            jl = 2 * (jof[C_LR] % 2)
            act.activation(two(lrT), ps[0:RANK, jl:jl + 2, 0:HALF], ACT.Copy).then_inc(frees(C_LR), 1)
            key_gates(0)
            query_gate(0)
            decays(0)
            take_values(C_BV, AH * ADV)
            for u in range(NU):
                turned_keys(u)
                if u > 0:
                    head_hi(u - 1, last(u - 1))
                if u + 1 < NU:
                    key_gates(u + 1)
                    query_gate(u + 1)
                    decays(u + 1)
                for step in (head_out, out_gate) if u + 1 < NU else (out_gate, head_out):
                    step(u, 0)
                states(u)
                if last(u):
                    head_out(u, 1)
                    head_hi(u, 0)
                    out_gate(u, 1)
            head_hi(NU - 1, last(NU - 1))
            ahead(C_O0 - 1)
            assert hp[0] == C_O0 + LEAD
            for m in range(KT):
                hi(C_O0 + m + LEAD)
                next_x(1, C_O0, m)
            rms(1)
            ffn(0)
            def take(c, dst):
                ahead(c)
                wait_done(act, c)
                act.activation(dst.rearrange("p (h t) -> p h t", h=2), pair(c), ACT.Copy).then_inc(frees(c), 1)

            def relus(n):
                m = P if n < 3 else TS
                for h in range(4):
                    act.wait_ge(sc_done, 4 * n + h + 1)
                    if n > 0:
                        act.wait_ge(sc_acc, 4 * (n - 1) + h + 1)
                    act.activation(relu[0:m, h, 0:nks[n]], ps[0:m, 4 + h, 0:nks[n]], ACT.Relu, scale=1.0 / 16.0).then_inc(sc_relu, 1)

            def out_tm(name, src):
                for pre, s, n in (("p_", src[:, 0:NT], TP), ("s_", src[0:TS, NT], TS)):
                    dst = O[pre + name][0, 0]
                    if len(dst.shape) == 3:
                        dst = dst.rearrange("t h n -> t (h n)")
                    if n == TP:
                        dst = dst.rearrange("(i p) n -> p i n", p=P)
                    act.dma_start(dst, s).then_inc(m1_out, 16)

            def take_keys(dst, n, base):
                for i in range(NT + 1):
                    m = P if i < NT else TS
                    act.wait_ge(k_turned, base + i + 1)
                    act.activation(dst[0:m, i, 0:n], ps[0:m, 4 + i % 4, 0:n], ACT.Copy).then_inc(k_taken, 1)
                act.wait_ge(k_taken, base + NT + 1)

            def attention(dsa):
                X0, PX = NX * dsa, 5 * dsa

                def exps(x):
                    act.wait_ge(at_mx, X0 + x + 1)
                    if x >= 3:
                        act.wait_ge(at_t, X0 + x - 2)
                    for j, (i, c, nk) in enumerate(groups[x][1] or [(NT, 0, KS)]):
                        ins = act.activation(prob[:, x % 3, c:c + nk], ps[:, x % 4, c:c + nk], ACT.Exp, bias=nmx[:, x % 4, j:j + 1],
                                             scale=1.0 / 8.0, accum_out=psums[:, x % 4, j:j + 1])
                    ins.then_inc(at_e, 1)

                def copies(x):
                    act.wait_ge(at_t, X0 + x + 1)
                    if x >= 2:
                        act.wait_ge(at_v, X0 + x - 1)
                    tiles = groups[x][1]
                    b = ps[:, 4 + x % 2, :]
                    if tiles is None:
                        act.activation(pt[x % 2][:, 0:2 * P], b[:, 0:2 * P], ACT.Copy)
                        act.activation(pt[x % 2][0:TS, 2 * P:3 * P], b[0:TS, 2 * P:3 * P], ACT.Copy).then_inc(at_c, 1)
                    else:
                        n = tiles[-1][1] + tiles[-1][2]
                        act.activation(pt[x % 2][:, 0:n], b[:, 0:n], ACT.Copy).then_inc(at_c, 1)

                def outputs(x):
                    pi = pairs_end.index(x)
                    act.wait_ge(at_v, X0 + x + 1)
                    b = ps[:, 6 + (PX + pi) % 2, :]
                    if pi < 4:
                        act.activation(oh[:, 4 * dsa + pi, 0:TP], b, ACT.Copy).then_inc(at_h, 1)
                    else:
                        act.activation(oh[:, 4 * dsa:4 * dsa + 4, TP:T], b[:, 0:4 * TS].rearrange("p (t n) -> p t n", t=4), ACT.Copy)\
                           .then_inc(at_h, 1)

                exps(0)
                exps(1)
                for x in range(NX + 2):
                    if x + 2 < NX:
                        exps(x + 2)
                    if x < NX:
                        copies(x)
                    if x - 2 in pairs_end:
                        outputs(x - 2)

            hp[0] = C_M1 + LEAD
            for c in range(C_M1, C_M1 + 4):
                ahead(c)
            rms(2, 2 * (jof["norm"] % 2))
            wait_done(act, C_M1 + 3)
            for i in [NT] + list(range(NT)):
                m, b = (P, 4 + i) if i < NT else (TS, 2 * (jof[C_M1] % 2))
                act.activation(dv[0:m, i, :], ps[0:m, b, 0:P], ACT.Copy, scale=rcol[0:m, i:i + 1])
                act.activation(stage[0:m, i, :], ps[0:m, b, P:TBW], ACT.Copy, scale=rcol[0:m, i:i + 1]).then_inc(tb_out if i < NT else frees(C_M1), 1)
            ahead(C_CK[0])
            act.wait_ge(lf_biased, 2)
            for n, (m, i0, i1) in enumerate(token_tiles):
                a_ = lf_a[0:m, i0:i1]
                ch.link(act.activation(a_, lf_z[0:m, i0:i1], ACT.Abs))
                ch.link(act.activation(a_, a_, ACT.Exp, scale=-1.0))
                act.activation(a_, a_, ACT.Ln, bias=ones[0:m, 0:1]).then_inc(lf_abs, 1)
            out_tm("dsa_v", dv)
            out_tm("dsa_ik", stage[:, :, 4 * IDX:5 * IDX])
            take(C_CK[0], kT[:, 0])
            act.wait_ge(lf_ready, 2)
            out_tm("fox_logf", lft)
            for r, parts in enumerate([[(0, 0, P, iqT[:, 0]), (1, 0, P, iqT[:, 1])], [(0, 0, IDX, ikT), (1, IDX, P, ikT)]]):
                act.wait_ge(i_turned, r + 1)
                if r == 1:
                    act.wait_ge(lf_turned, 1)
                    for n0, b, o, m in ((0, 4, 2 * P, 2 * P), (2 * P, 6, 2 * P, 2 * P), (TP + PAST, 5, 2 * P + TS, TS)):
                        act.activation(lf[:, n0:n0 + m], ps[0:CH, b, o:o + m], ACT.Copy).then_inc(lf_out, 1)
                for n, p0, p1, dst in parts:
                    for b, n0, n1 in split:
                        act.activation(dst[p0:p1, n0:n1], ps[p0:p1, 4 + 2 * n + b, 0:n1 - n0], ACT.Copy).then_inc(i_out, 1)
                take(C_CK[r + 1], kT[:, r + 1])
            relus(0)
            take(C_CK[3], kT[:, 3])
            relus(1)
            act.wait_ge(cp_done, 1)
            take(C_CQ[0], qT[:, 0])
            relus(2)
            take(C_CQ[1], qT[:, 1])
            relus(3)
            for c in range(C_CV, C_CV + 4):
                ahead(c)
            wait_done(act, C_CV + 3)
            act.wait_ge(sc_acc, 16)
            for i in range(NT + 1):
                m, b = (P, 4 + i) if i < NT else (TS, 2 * (jof[C_CV] % 2))
                act.activation(cv[0:m, i, :], ps[0:m, b, :], ACT.Copy, scale=rcol[0:m, i:i + 1]).then_inc(cv_out if i < NT else frees(C_CV), 1)
            act.wait_ge(cv_out, NT)
            act.wait_ge(frees(C_CV), jof[C_CV] // 2 + 1)
            out_tm("fox_v", cv)
            take(C_CQ[2], qT[:, 2])
            take(C_CQ[3], qT[:, 3])
            act.wait_ge(m1_out, 16 * 8)
            take_keys(k_out, CH * HD, 0)
            out_tm("fox_k", k_out)
            attention(0)
            for c in [C_DK] + C_DQ:
                ahead(c)
            act.wait_ge(m1_out, 16 * 10)
            take_keys(k_out[:, :, 0:P], P, NT + 1)
            out_tm("dsa_k", k_out[:, :, 0:P])
            attention(1)
            ahead(C_O1 - 1)
            act.wait_ge(m1_out, 16 * 12)
            assert hp[0] == C_O1 + LEAD
            for m in range(KT):
                hi(C_O1 + m + LEAD)
                next_x(3, C_O1, m)
            rms(3)
            ffn(1)
            rms(4)

        @block.tensor
        def _(pe):
            PASSES = ((wh, 0), (wh, 1), (wl, 0))

            def wait_pair(j, jx=0):
                if j >= 2 or not isinstance(jx, int):
                    pe.wait_ge(pair_free[j % 2], j // 2 + jx)

            def job(c, xs, it=0, n=KT, M=P, ready=None, ks=None, begin=True, end=True):
                if begin:
                    pe.wait_ge(lo_done, c + 1 + 4 * it)
                    wait_pair(jof[c], 2 * it)
                s, b = c % SLOTS, 2 * (jof[c] % 2)
                ks = ks or list(range(n))
                for k in ks:
                    if ready is not None:
                        ready(k)
                    for a, (w, x) in enumerate(PASSES):
                        for h in range(2):
                            mm = pe.matmul(ps[0:M, b + h, 0:HALF], w[:, s, k * M:(k + 1) * M],
                                           xs[x][:, k, h * HALF:(h + 1) * HALF],
                                           start=(begin and k == ks[0] and a == 0), stop=(end and k == ks[-1] and a == 2))
                if end:
                    mm.then_inc(chunk_done, 1)

            pe.wait_ge(s_const, 3)
            pe.wait_ge(s_in, 16 * (NT + 1))
            for k in range(KT):
                wait_pair(k)
                b = 2 * (k % 2)
                for i in range(NT):
                    pe.transpose(ps[:, b, i * P:(i + 1) * P], x_in[:, i, k * P:(k + 1) * P], ident[:, :])
                pe.transpose(ps[:, b + 1, 0:TS], xs_in[:, k * P:(k + 1) * P], ident[0:TS, 0:TS]).then_inc(x_turned, 1)

            def first_norm():
                pe.wait_ge(s_par, 16 * len(rows))
                pe.transpose(ps[:, 5, 0:NPR], par_in[0:NPR, :], ident[0:NPR, 0:NPR]).then_inc(s_part, 1)
                norm(0)

            def norm(n, b=6):
                pe.wait_ge(s_acc, (KT - 1) * (n + 1))
                if n < 4:
                    for h in range(2):
                        mm = pe.matmul(ps[:, b + h, 0:HALF], ones[:, :], acc[:, h * HALF:(h + 1) * HALF], start=True, stop=True)
                if n in (2, 4):
                    for i in range(NT + 1):
                        m = P if i < NT else TS
                        mm = pe.matmul(ps[0:m, b, HALF + i:HALF + i + 1], acc[:, i * P:i * P + m], ones[:, 0:1],
                                       start=True, stop=True)
                mm.then_inc(s_ss, 1)

            def xready(n):
                return lambda k: pe.wait_ge(s_nl, KT * n + k + 1)

            def turn_caches():
                pe.wait_ge(s_const, 2)
                pe.wait_ge(s_m1in, 16 * 8)
                for t in range(4):
                    for i in range(2):
                        mm = pe.transpose(ps[:, 4 + t // 2, (t % 2) * PAST + i * P:(t % 2) * PAST + (i + 1) * P],
                                          ck_raw[:, i, t * P:(t + 1) * P], ident[:, :])
                mm.then_inc(c_turned, 1)
                for i in range(2):
                    pe.transpose(ps[:, 6, i * P:(i + 1) * P], dk_raw[:, i, :], ident[:, :])
                    pe.transpose(ps[:, 6, PAST + i * P:PAST + (i + 1) * P], ik_raw[:, i, :], ident[:, :])
                    mm = pe.transpose(ps[0:CH, 7, i * P:(i + 1) * P], lf_raw[:, i, :], ident[:, :])
                mm.then_inc(c_turned, 1)

            def ffn_part(l, cb, itp, hx, n, first=False, last=False):
                xr = xready(1 + 2 * l)
                if first:
                    job(cb, (xh, xl), itp, ready=xr)
                    norm(1 + 2 * l)
                    for k in range(1, 4):
                        job(cb + k, (xh, xl), itp, ready=xr)
                with pe.Fori(int(first), n // 2) as i:
                    for k in range(4):
                        job(cb + k, (xh, xl), itp + i, ready=xr)
                if last and l == 0:
                    turn_caches()
                with pe.Fori(0, 2) as i:
                    for k in range(4):
                        job(cb + 2 * n + k, (oh, ol), itp + i, n=n, ready=lambda k: pe.wait_ge(f_lo, FT * l + hx + k + 1))

            def ffn(l):
                for part in range(2):
                    ffn_part(l, C_F[l], part * 6, part * PART, PART, part == 0)
                ffn_part(l, C_F[l] + 48, 0, 2 * PART, FT - 2 * PART, last=True)

            def out_projection(c0, ready, m0=0):
                for m in range(m0, KT):
                    job(c0 + m, (oh, ol), ready=ready)

            first_norm()
            def tm_section(c0, N, ready=None, between=None):
                wait_pair(jof[c0])
                for q in range(KT // 2):
                    pe.wait_ge(lo_done, c0 + q + 1)
                    s = (c0 + q) % SLOTS
                    for kk in range(2):
                        k = 2 * q + kk
                        if ready is not None:
                            ready(k)
                        for i in range(NT + 1):
                            out = ps[:, 4 + i, 0:N] if i < NT else ps[0:TS, 2 * (jof[c0] % 2), 0:N]
                            for a, (w, x) in enumerate(PASSES):
                                mm = pe.matmul(out, (xh, xl)[x][:, k, i * P:min(T, (i + 1) * P)], w[:, s, kk * N:(kk + 1) * N],
                                               start=(k == 0 and a == 0), stop=(k == KT - 1 and a == 2))
                    mm.then_inc(chunk_done, 1)
                    if q == 0 and between is not None:
                        between()

            def key_jobs(u):
                kind, i, hs, s0 = unit(u)
                if kind == "b":
                    j = jof["gk", u]
                    wait_pair(j)
                    wait_freed(pe, C_LR)
                    for h in range(2):
                        mm = pe.matmul(ps[:, 2 * (j % 2) + h, 0:HALF], wgk[:, i * P:(i + 1) * P],
                                       lrT[:, h * HALF:(h + 1) * HALF], start=True, stop=True)
                    mm.then_inc(gk_done, 1)
                job(c_key[u], (xh, xl))

            def at(b, n0, n1):
                k = int(n0 >= 2 * P)
                return ps[:, b + k, n0 - 2 * P * k:n1 - 2 * P * k]

            def scores(u, e, b):
                ko, kz, vc, hd = unit(u)[2][e]
                for t in range(NT + 1):
                    n0, n1 = t * P, min(T, (t + 1) * P)
                    mm = pe.matmul(at(b, n0, n1)[0:n1 - n0], kp[ko:ko + kz, u % 2, n0:n1], qp[ko:ko + kz, u % 2, n0:n1],
                                   start=True, stop=True)
                mm.then_inc(r_att, 1)

            def turn_and_score(u):
                pe.wait_ge(u_dve, UD[u + 1])
                if u > 0:
                    pe.wait_ge(r_r, (NB + 1) * u)
                else:
                    pe.wait_ge(s_val, NT + 2)
                for t in range(NT + 1):
                    n = P if t < NT else TS
                    b, o = (4, t * P) if t < 2 else (5, (t - 2) * P)
                    mm = pe.transpose(ps[0:n, b, o:o + P], kp[:, u % 2, t * P:t * P + n], ident[:, :])
                mm.then_inc(r_kt, 1)
                if u == 0:
                    pe.wait_ge(s_val, 2 * NT)
                scores(u, 0, 6)
                if last(u):
                    wait_pair(jof["score", u])
                    scores(u, 1, 2 * (jof["score", u] % 2))

            def update(u, n, out):
                for ko, kz, vc, hd in unit(u)[2]:
                    q = n % 4 * BLK
                    mm = pe.matmul(out[ko:ko + kz], ktm[q:q + BLK, n // 4, ko:ko + kz], val[q:q + BLK, n // 4, vc:vc + ADV],
                                   start=True, stop=True)
                return mm

            def updates(u):
                wait_freed(pe, C_BV)
                pe.wait_ge(r_ktm, 3 * (u + 1))
                pe.wait_ge(r_attm, 3 * (u + 1))
                for q in range(4):
                    for t in range(NT):
                        mm = update(u, 4 * t + q, ps[:, 4 + q, t * P:(t + 1) * P])
                    mm.then_inc(r_w, 1)

            def outputs(u):
                kind, i, hs, s0 = unit(u)
                base = (NB + 1) * u
                pe.wait_ge(r_r, base + NB - 3)
                update(u, NB, ps[:, 4, 0:P]).then_inc(r_w, 1)
                pe.wait_ge(r_r, base + NB)
                for e, (ko, kz, vc, hd) in enumerate(hs):
                    ob = obank(e)
                    if e:
                        wait_freed(pe, ("score", u))
                        pe.wait_ge(r_r, base + NB + 1)
                    for t in range(NT + 1):
                        n0, n1 = t * P, min(T, (t + 1) * P)
                        out = ps[0:n1 - n0, ob + t // NT, t % NT * P:(t % NT + 1) * P]
                        mm = pe.matmul(out, att[0:n1 - n0, e, n0:n1], val[0:n1 - n0, t, vc:vc + ADV],
                                       start=(t % NT == 0), stop=False, skip_group_check=True)
                    if e:
                        mm.then_inc(r_intra, 1)
                        pe.wait_ge(r_intra, units[u][1] + 1)
                    for n in range(1, NB + 1):
                        t, o = n // 4, n % 4 * BLK
                        st = rst[ko:ko + kz, n - 1, :] if n < NB else s0[ko:ko + kz, :]
                        mm = pe.matmul(ps[o:o + BLK, ob + t // NT, t % NT * P:(t % NT + 1) * P],
                                       q2[ko:ko + kz, u % 2, n * BLK:(n + 1) * BLK], st,
                                       start=False, stop=True, skip_group_check=True, tile_position=(ko, o))
                    mm.then_inc(r_o, 1)

            def turn_outputs(u, e):
                j = jof["turn", u, e]
                pe.wait_ge(r_tm, 2 * (heads_before[u] + e + 1))
                wait_pair(j)
                for t in range(NT + 1):
                    n0, n1 = t * P, min(T, (t + 1) * P)
                    mm = pe.transpose(at(2 * (j % 2), n0, n1), ktm[0:n1 - n0, t, :], ident[0:n1 - n0, 0:n1 - n0])
                mm.then_inc(r_ot, 1)

            X0 = (xh, xl)
            pe.wait_ge(s_part, 2)
            tm_section(0, AH * ADV, ready=xready(0))
            job(C_LR, X0, M=RANK)
            pe.wait_ge(s_m0in, 64)
            key_jobs(0)
            job(c_query[0], X0)
            pe.wait_ge(s_val, NT)
            tm_section(C_BV, BH * BDV)
            for u in range(NU):
                more, g = u + 1 < NU, list(c_gates[u])
                turn_and_score(u)
                if more:
                    key_jobs(u + 1)
                updates(u)
                job(c_query[u + 1] if more else g.pop(0), X0)
                outputs(u)
                if not more:
                    heads = [k for k in range(KT) if k != unit(u)[2][0][3]]
                    job(C_O0, (oh, ol), ready=lambda k: pe.wait_ge(o_lo, KT - 1), ks=heads, end=False)
                for e in range(last(u) + 1):
                    if g:
                        job(g.pop(0), X0)
                    turn_outputs(u, e)
            job(C_O0 + 1, (oh, ol), ks=heads, end=False)
            pe.wait_ge(o_lo, KT)
            for c in (C_O0, C_O0 + 1):
                job(c, (oh, ol), ks=[unit(NU - 1)[2][0][3]], begin=False)
            out_projection(C_O0, lambda k: None, 2)
            ffn(0)
            def turn_idx(cols4):
                for n, (c0, m) in enumerate(cols4):
                    for i in range(NT + 1):
                        b, o = 4 + 2 * n + i // 2 if i < NT else 5 + 2 * n, (i % 2) * P if i < NT else 2 * P
                        w_ = P if i < NT else TS
                        mm = pe.transpose(ps[0:m, b, o:o + w_], stage[0:w_, i, c0:c0 + m], ident[0:w_, 0:w_])
                mm.then_inc(i_turned, 1)

            def scores(n):
                if n == 0:
                    pe.wait_ge(i_out, 8)
                    pe.wait_ge(lf_out, 3)
                q0, m = ((n + 1) * P, P) if n < 3 else (TP, TS)
                for h in range(4):
                    if n > 0:
                        pe.wait_ge(sc_relu, 4 * (n - 1) + h + 1)
                    r0, a = (h % 2) * IDX, h // 2
                    q = iqT[r0:r0 + IDX, a, q0:q0 + m]
                    if n < 3:
                        mm = pe.matmul(ps[0:m, 4 + h, 0:nks[n]], q, ikT[r0:r0 + IDX, 0:nks[n]], start=True, stop=True)
                    else:
                        pe.matmul(ps[0:m, 4 + h, 0:PAST], q, ikc[r0:r0 + IDX, :], start=True, stop=True)
                        mm = pe.matmul(ps[0:m, 4 + h, PAST:KS], q, ikT[r0:r0 + IDX, TP:T], start=True, stop=True)
                    mm.then_inc(sc_done, 1)

            def attention(dsa):
                X0, PX = NX * dsa, 5 * dsa
                v, vc_ = (dv, dvc) if dsa else (cv, cvc)

                def heads_of(x):
                    h, tiles = groups[x]
                    out = []
                    for k in ([h] if tiles is not None else range(4 * h, 4 * h + 4)):
                        t, e = k // 2, k % 2
                        r = slice(e * HD, (e + 1) * HD)
                        c0 = e * HD if dsa else k * HD
                        out.append((k, t, e, kT[r, 0 if dsa else t, :], dkc[r, :] if dsa else ckc[r, t, :], slice(c0, c0 + HD), 32 * (k % 4)))
                    return out

                def masks(x):
                    h, tiles = groups[x]
                    L = ps[:, x % 4, :]
                    if x >= 4:
                        pe.wait_ge(at_e, X0 + x - 3)
                    if tiles is None:
                        for k, t, e, _, _, _, o in heads_of(x):
                            if dsa:
                                mm = pe.matmul(L[o:o + 32, 0:KS], identb[0:TS, 0:TS], mb[4][0:TS, :], start=True, stop=False,
                                               skip_group_check=True, tile_position=(0, o))
                            else:
                                pe.matmul(L[o:o + 32, 0:KS], sel[0:96, k, 0:TS], cp[0:96, TP:W], start=True, stop=False,
                                          skip_group_check=True, tile_position=(0, o))
                                mm = pe.matmul(L[o:o + 32, PAST:KS], identb[0:TS, 0:TS], caus[0:TS, 0:TS], start=False, stop=False,
                                               skip_group_check=True, tile_position=(0, o))
                    else:
                        for i, o, nk in tiles:
                            if dsa:
                                mm = pe.matmul(L[:, o:o + nk], identb[:, :], mb[i], start=(o == 0), stop=False, skip_group_check=True)
                            else:
                                pe.matmul(L[:, o:o + nk], sel[0:96, h, :], cp[0:96, 0:nk], start=(o == 0), stop=False, skip_group_check=True)
                                mm = pe.matmul(L[:, o + i * P:o + nk], identb[:, :], caus, start=False, stop=False, skip_group_check=True)
                    mm.then_inc(at_m, 1)

                def logits(x):
                    h, tiles = groups[x]
                    L = ps[:, x % 4, :]
                    pe.wait_ge(at_m, X0 + x + 1)
                    for k, t, e, ks_, kc_, _, o in heads_of(x):
                        q = qT[e * HD:(e + 1) * HD, t, :]
                        if tiles is None:
                            pe.matmul(L[o:o + 32, 0:PAST], q[:, TP:T], kc_, start=False, stop=True, skip_group_check=True,
                                      tile_position=(e * HD, o))
                            mm = pe.matmul(L[o:o + 32, PAST:KS], q[:, TP:T], ks_[:, TP:T], start=False, stop=True,
                                           skip_group_check=True, tile_position=(e * HD, o))
                        else:
                            for i, c, nk in tiles:
                                mm = pe.matmul(L[:, c:c + nk], q[:, i * P:(i + 1) * P], ks_[:, 0:nk], start=False, stop=True,
                                               skip_group_check=True)
                    mm.then_inc(at_l, 1)

                def turn(x):
                    pe.wait_ge(at_p, X0 + x + 1)
                    if x >= 2:
                        pe.wait_ge(at_c, X0 + x - 1)
                    tiles = groups[x][1]
                    n = KS if tiles is None else tiles[-1][1] + tiles[-1][2]
                    for c in range(0, n, P):
                        m = min(P, n - c)
                        mm = pe.transpose(ps[0:m, 4 + x % 2, c:c + P], prob[:, x % 3, c:c + m], ident[:, :])
                    mm.then_inc(at_t, 1)

                def values(x):
                    pi = [n for n, last in enumerate(pairs_end) if x <= last][0]
                    if pi + PX >= 2:
                        pe.wait_ge(at_o, PX + pi - 1)
                    pe.wait_ge(at_c, X0 + x + 1)
                    tiles = groups[x][1]
                    for k, t, e, _, _, vcol, o in heads_of(x):
                        out = ps[e * HD:(e + 1) * HD, 6 + (PX + pi) % 2, :]
                        if tiles is None:
                            for kb in range(3):
                                vv = v[0:TS, NT, vcol] if kb == 2 else vc_[:, kb, vcol]
                                m = TS if kb == 2 else P
                                mm = pe.matmul(out[:, t * TS:(t + 1) * TS], vv, pt[x % 2][0:m, kb * P + o:kb * P + o + TS],
                                               start=(kb == 0), stop=(kb == 2), skip_group_check=True)
                        else:
                            for i, c, nk in tiles:
                                for kb in range(i + 1):
                                    mm = pe.matmul(out[:, i * P:(i + 1) * P], v[:, kb, vcol], pt[x % 2][:, c + kb * P:c + (kb + 1) * P],
                                                   start=(kb == 0), stop=(kb == i), skip_group_check=True)
                    mm.then_inc(at_v, 1)

                for x in range(3):
                    masks(x)
                    logits(x)
                for x in range(NX + 1):
                    if x + 3 < NX:
                        masks(x + 3)
                    if x < NX:
                        turn(x)
                    if x + 3 < NX:
                        logits(x + 3)
                    if x >= 1:
                        values(x - 1)

            def turn_keys(src, base):
                for i in range(NT + 1):
                    n = P if i < NT else TS
                    if i == NT:
                        pe.wait_ge(k_taken, base + 1)
                    for t in range(len(src)):
                        mm = pe.transpose(ps[0:n, 4 + i % 4, t * P:(t + 1) * P], src[t][:, i * P:i * P + n], ident[:, :])
                    mm.then_inc(k_turned, 1)

            X1 = (xh, xl)
            pe.wait_ge(c_out, 5)


            def mixer_norm():
                wait_pair(jof["norm"])
                norm(2, 2 * (jof["norm"] % 2))

            tm_section(C_M1, TBW, ready=xready(2), between=mixer_norm)
            job(C_CK[0], X1)
            pe.wait_ge(tb_out, NT)
            turn_idx([(0, P), (P, P)])
            job(C_CK[1], X1)
            pe.wait_ge(i_out, 4)
            turn_idx([(4 * IDX, IDX), (3 * IDX, P)])
            pe.wait_ge(lf_ready, 2)
            for i in range(NT + 1):
                n = P if i < NT else TS
                b, o = (4 + i // 2 * 2, (2 + i % 2) * P) if i < NT else (5, 2 * P + TS)
                mm = pe.transpose(ps[0:CH, b, o:o + n], lft[0:n, i, :], ident[0:n, 0:n])
            mm.then_inc(lf_turned, 1)
            job(C_CK[2], X1)
            scores(0)
            job(C_CK[3], X1)
            scores(1)
            job(C_CQ[0], X1)
            scores(2)
            job(C_CQ[1], X1)
            scores(3)
            pe.wait_ge(sc_relu, 16)
            tm_section(C_CV, CH * HD)
            job(C_CQ[2], X1)
            job(C_CQ[3], X1)
            pe.wait_ge(cv_out, NT)
            pe.wait_ge(k_scaled, 4)
            turn_keys([kT[:, t, :] for t in range(4)], 0)
            wait_freed(pe, C_CQ[3])
            wait_freed(pe, C_CQ[2])
            pe.wait_ge(k_taken, NT + 1)
            pe.wait_ge(k_scaled, 8)
            pe.wait_ge(cp_done, 1)
            pe.wait_ge(s_m1c, 3)
            attention(0)
            pe.wait_ge(at_e, NX)
            job(C_DK, X1)
            for t in range(4):
                job(C_DQ[t], X1)
            pe.wait_ge(at_o, 5)
            wait_freed(pe, C_DK)
            turn_keys([kT[:, 0, :]], NT + 1)
            wait_freed(pe, C_DQ[3])
            wait_freed(pe, C_DQ[2])
            pe.wait_ge(k_taken, 2 * (NT + 1))
            attention(1)
            pe.wait_ge(at_e, 2 * NX)
            out_projection(C_O1, lambda k: pe.wait_ge(at_o, 10))
            ffn(1)
            for i in range(NT + 1):
                n = P if i < NT else TS
                if i == 0:
                    pe.wait_ge(x_scaled, KT)
                if i == 2:
                    norm(4)
                if i >= 2:
                    pe.wait_ge(y_ready, i - 1)
                for k in range(KT):
                    mm = pe.transpose(ps[0:n, 2 * (i % 2) + k // 4, (k % 4) * P:(k % 4 + 1) * P],
                                      x_out[:, k, i * P:i * P + n], ident[:, :])
                mm.then_inc(y_turned, 1)

        @block.vector
        def _(dve):
            ch = Chain(dve, dve_s)

            def add_square(n, m):
                dve.wait_ge(s_sq, KT * n + m + 1)
                if m > 1:
                    dve.wait_ge(s_acc, (KT - 1) * n + m - 1)
                dve.tensor_tensor(acc, acc, sq2[:, m % 2, :], ALU.add).then_inc(s_acc, 1)

            for k in range(KT):
                dve.wait_ge(x_turned, k + 1)
                b = 2 * (k % 2)
                dve.tensor_copy(xT[:, k, 0:TP], ps[:, b, :])
                dve.tensor_copy(xT[:, k, TP:T], ps[:, b + 1, 0:TS]).then_inc(pair_free[k % 2], 1)
                if k > 1:
                    add_square(0, k - 1)
            add_square(0, KT - 1)

            def first_norm():
                def lo_part(k):
                    dve.wait_ge(s_nh, k + 1)
                    dve.tensor_tensor(xl[:, k, :], ntmp[:, k % NR, :], xh[:, k, :].bitcast(F32), ALU.subtract).then_inc(s_nl, 1)

                dve.wait_ge(s_part, 1)
                dve.tensor_copy(par[:, 0:NPR], ps[:, 5, 0:NPR]).then_inc(s_part, 1)
                dve.wait_ge(s_part, 2)
                dve.wait_ge(s_rs, 1)
                for k in range(KT):
                    if k >= NR:
                        dve.wait_ge(s_nl, k - NR + 1)
                    dve.scalar_tensor_tensor(out=ntmp[:, k % NR, :], in0=xT[:, k, :], scalar=pc("mix0", k), in1=rstd[:, :],
                                             op0=ALU.mult, op1=ALU.mult).then_inc(s_nt, 1)
                    if k >= 1:
                        lo_part(k - 1)
                lo_part(KT - 1)

            def add_back(n, c0):
                def rest(m):
                    if n < 4:
                        dve.wait_ge(s_nh, KT * n + m + 1)
                        dve.scalar_tensor_tensor(out=xl[:, m, :], in0=xT[:, m, :], scalar=pc(norm_names[n], m),
                                                 in1=xh[:, m, :].bitcast(F32), op0=ALU.mult, op1=ALU.subtract).then_inc(s_nl, 1)
                    if m > 0:
                        add_square(n, m)

                for m in range(KT):
                    wait_done(dve, c0 + m)
                    dve.tensor_tensor(two(xT[:, m, :]), pair(c0 + m), two(xT[:, m, :]), ALU.add).then_inc(frees(c0 + m), 1)
                    if n == 4:
                        wait_freed(dve, c0 + m)
                        dve.tensor_scalar(x_out[:, m, :], xT[:, m, :], pc("final", m), None, ALU.mult).then_inc(x_scaled, 1)
                    if m > 0:
                        rest(m - 1)
                rest(KT - 1)

            def take_caches():
                dve.wait_ge(c_turned, 1)
                for t in range(0, 4, 2):
                    dve.tensor_copy(ckc[:, t:t + 2, :], ps[:, 4 + t // 2, :].rearrange("p (t k) -> p t k", t=2)).then_inc(c_out, 1)
                dve.wait_ge(c_turned, 2)
                dve.tensor_copy(dkc, ps[:, 6, 0:PAST]).then_inc(c_out, 1)
                dve.tensor_copy(ikc, ps[:, 6, PAST:2 * PAST]).then_inc(c_out, 1)
                dve.tensor_copy(lf[:, TP:TP + PAST], ps[0:CH, 7, 0:PAST]).then_inc(c_out, 1)

            def ffn_part(l, cb, itp, hx, n, last=False):
                with dve.Fori(0, n // 2) as i:
                    it = itp + i
                    for k in range(2):
                        h = FT * l + hx + 2 * i + k + 1
                        g, u = cb + 2 * k, cb + 2 * k + 1
                        fgk = fg[:, k, :]
                        dve.wait_ge(s_rs, 2 * l + 2)
                        wait_done(dve, g, it)
                        dve.tensor_tensor(two(fgk), pair(g), two(rstd[:, :]), ALU.mult).then_inc(frees(g), 1)
                        dve.wait_ge(f_sig, h)
                        dve.tensor_tensor(fgk, fgk, fsig[:, k, :], ALU.mult).then_inc(f_mul, 1)
                        dve.wait_ge(f_mul, h * 2 - 1)
                        dve.tensor_tensor(fgk, fgk, rstd[:, :], ALU.mult).then_inc(f_mul, 1)
                        wait_done(dve, u, it)
                        dve.wait_ge(f_mul, h * 2)
                        dve.tensor_tensor(two(fh[:, k, :]), two(fgk), pair(u), ALU.mult).then_inc(frees(u), 1)
                        dve.wait_ge(f_hi, h)
                        hid = bass.ds(i * 2 + k, 1)
                        dve.tensor_tensor(ol[:, hid, :], fh[:, k:k + 1, :], oh[:, hid, :].bitcast(F32), ALU.subtract)\
                           .then_inc(f_lo, 1)
                if last and l == 0:
                    take_caches()
                if last:
                    add_back(2 * l + 2, cb + 2 * n)
                    return
                with dve.Fori(0, 2) as i:
                    for k in range(4):
                        c = cb + 2 * n + k
                        wait_done(dve, c, itp + i)
                        xv = xT[:, bass.ds(i * 4 + k, 1), :].rearrange("p k (h t) -> p (k h) t", h=2)
                        dve.tensor_tensor(xv, pair(c), xv, ALU.add).then_inc(frees(c), 1)

            def ffn(l):
                with dve.Fori(0, 2) as part:
                    ffn_part(l, C_F[l], part * 6, part * PART, PART)
                ffn_part(l, C_F[l] + 48, 0, 2 * PART, FT - 2 * PART, last=True)

            first_norm()
            blocks = lambda ap: ap.rearrange("p (n l) -> p n l", l=BLK)
            c3 = lambda ap: ap.rearrange("p (n o) -> p n o", o=1)

            def key_gates(u):
                kind, i, hs, s0 = unit(u)
                c0, d0, a0 = c_key[u], UD[u], UA[u]
                if kind == "a":
                    wait_freed(dve, c0)
                    dve.tensor_scalar(t2, t1, oml[:, i:i + 1], lb[:, i:i + 1], ALU.mult, ALU.add).then_inc(u_dve, 1)
                    dve.wait_ge(u_dve, d0 + 1)
                    dve.tensor_scalar(t1, t2, -1.0, 1.0, ALU.mult, ALU.add).then_inc(u_dve, 1)
                else:
                    key = ("gk", u)
                    dve.wait_ge(u_act, a0 + 1)
                    dve.tensor_scalar(two(t4), pair(key), pc("bgk", i), 0.0, ALU.add, ALU.min).then_inc(frees(key), 1)
                    wait_freed(dve, key)
                    dve.tensor_tensor(t2, t4, t1, ALU.subtract).then_inc(u_dve, 1)

            def decays(u):
                kind, d0, a0, p = units[u][0], UD[u], UA[u], PRE[units[u][0]]
                dve.wait_ge(u_act, a0 + 1)
                dve.wait_ge(u_dve, d0 + p)
                dve.wait_ge(s_m0c, 2)
                dve.tensor_tensor_scan(t3, smask[:, :], t2, 0.0, ALU.mult, ALU.add).then_inc(u_dve, 1)
                dve.wait_ge(u_dve, d0 + p + 1)
                b = blocks(t3)
                mid, end = b[:, :, MID:MID + 1], b[:, :, BLK - 1:BLK]
                dve.tensor_tensor(blocks(t2), b, mid.broadcast_to([P, NB + 1, BLK]), ALU.subtract).then_inc(u_dve, 1)
                dve.tensor_tensor(c3(tail_), end, mid, ALU.subtract).then_inc(u_dve, 1)
                dve.tensor_copy(c3(ee), mid).then_inc(u_dve, 1)
                dve.wait_ge(u_dve, d0 + p + 4)
                dve.tensor_tensor(ee[:, 1:NB], ee[:, 1:NB], tail_[:, 0:NB - 1], ALU.add).then_inc(u_dve, 1)

            def keys(u):
                if u >= 2:
                    dve.wait_ge(r_o, heads_before[u - 1])
                dve.wait_ge(u_act, UA[u + 1])
                if units[u][0] == "a":
                    dve.tensor_tensor(kp[:, u % 2, :], t1, t2, ALU.mult).then_inc(u_dve, 1)
                else:
                    wait_done(dve, c_key[u])
                    dve.tensor_tensor(two(kp[:, u % 2, :]), two(t2), pair(c_key[u]), ALU.mult).then_inc(frees(c_key[u]), 1)

            def queries(u):
                r, cq = u % 2, c_query[u]
                wait_done(dve, cq)
                if units[u][0] == "a":
                    dve.wait_ge(u_act, UA[u] + 2)
                    dve.tensor_tensor(two(qp[:, r, :]), two(t4), pair(cq), ALU.mult).then_inc(frees(cq), 1)
                    wait_freed(dve, cq)
                    dve.tensor_tensor(qp[:, r, :], qp[:, r, :], t3, ALU.mult).then_inc(q_decayed, 1)
                    dve.wait_ge(q_decayed, units[u][1] + 1)
                else:
                    dve.scalar_tensor_tensor(out=two(qp[:, r, :]), in0=pair(cq), scalar=BDK ** -0.5, in1=two(t3),
                                             op0=ALU.mult, op1=ALU.mult).then_inc(frees(cq), 1)
                    wait_freed(dve, cq)
                dve.tensor_tensor(blocks(q2[:, r, :]), blocks(qp[:, r, :]), c3(ex[r]).broadcast_to([P, NB + 1, BLK]), ALU.mult)\
                   .then_inc(u_dve, 1)

            def out_gate(u, e):
                c = c_gates[u][e]
                dve.wait_ge(gate_sig, heads_before[u] + e + 1)
                dve.tensor_tensor(two(gate[:, e, :]), two(gate[:, e, :]), pair(c), ALU.mult).then_inc(frees(c), 1)

            def mask_scores(u, e):
                dve.wait_ge(r_att, heads_before[u] + e + 1)
                pm = matt[:, :].bitcast(U32)
                tiles = lambda ap: ap.rearrange("p (i l) -> p i l", l=P)
                b0 = 2 * (jof["score", u] % 2) if e else 6
                for b in range(2):
                    dve.copy_predicated(tiles(att[:, e, 2 * b * P:2 * (b + 1) * P]),
                                        pm.rearrange("p (o l) -> p o l", o=1).broadcast_to([P, 2, P]),
                                        tiles(ps[:, b0 + b, 0:2 * P])).then_inc(att_parts if e else r_attm, 1)
                dve.copy_predicated(att[0:TS, e, TP:T], pm[0:TS, 0:TS], ps[0:TS, b0 + 1, 2 * P:2 * P + TS])\
                   .then_inc(frees(("score", u)) if e else r_attm, 1)

            def states(u):
                for n in range(NB):
                    dve.wait_ge(r_w, NW * u + min(n + 1, 4))
                    w = ps[:, 4 + n % 4, n // 4 * P:(n // 4 + 1) * P]
                    if n == 0:
                        dve.tensor_copy(rst[:, 0, :], w).then_inc(r_r, 1)
                    else:
                        dve.wait_ge(r_r, (NB + 1) * u + n)
                        dve.scalar_tensor_tensor(out=rst[:, n, :], in0=rst[:, n - 1, :], scalar=ex[u % 2][:, n:n + 1], in1=w,
                                                 op0=ALU.mult, op1=ALU.add).then_inc(r_r, 1)

            def final_states(u):
                dve.wait_ge(r_w, NW * u + 5)
                dve.scalar_tensor_tensor(out=rst[:, NB, :], in0=unit(u)[3], scalar=ex[u % 2][:, NB:NB + 1], in1=ps[:, 4, 0:P],
                                         op0=ALU.mult, op1=ALU.add).then_inc(r_r, 1)
                dve.wait_ge(r_r, (NB + 1) * (u + 1))
                for n in (NB - 1, NB):
                    dve.tensor_scalar(rst[:, n, :], rst[:, n, :], tx[:, u % 2, n:n + 1], None, ALU.mult).then_inc(state_final, 1)

            def head_norm(u, e):
                h, ob = heads_before[u] + e, obank(e)
                dve.wait_ge(r_ors, h + 1)
                dve.wait_ge(r_w, NW * (u + 1))
                for m, i0, i1 in token_tiles:
                    r = rss[e][0:m, i0:i1]
                    ch.add(dve.reciprocal(r, r))
                dve.wait_ge(dve_s, ch.n)
                if e:
                    dve.wait_ge(r_ot, h)
                by_value = lambda ap: ap.rearrange("p (t v) -> p t v", v=ADV)
                r = rss[e][:, 0:NT].rearrange("p (t o) -> p t o", o=1).broadcast_to([P, NT, ADV])
                dve.tensor_tensor(ktm[:, 0:NT, :], by_value(ps[:, ob, :]), r, ALU.mult).then_inc(r_tm, 1)
                dve.tensor_scalar(ktm[0:TS, NT, :], ps[0:TS, ob + 1, 0:P], rss[e][0:TS, NT:NT + 1], None, ALU.mult).then_inc(r_tm, 1)

            def head_gate(u, e):
                h, key = heads_before[u] + e, ("turn", u, e)
                dve.wait_ge(r_ot, h + 1)
                dve.wait_ge(o_lo, h)
                wait_freed(dve, c_gates[u][e])
                gn, b0 = pc("ga" if units[u][0] == "a" else "gb"), 2 * (jof[key] % 2)
                for b, n0, n1 in split:
                    ins = dve.scalar_tensor_tensor(out=osb[:, n0:n1], in0=ps[:, b0 + b, 0:n1 - n0], scalar=gn, in1=gate[:, e, n0:n1],
                                                   op0=ALU.mult, op1=ALU.mult)
                    if b == 0:
                        ch.add(ins)
                ins.then_inc(frees(key), 1)

            def head_lo(u, e):
                h = heads_before[u] + e
                dve.wait_ge(o_hi, h + 1)
                hd = unit(u)[2][e][3]
                wait_freed(dve, ("turn", u, e))
                dve.tensor_tensor(ol[:, hd, :], osb, oh[:, hd, :].bitcast(F32), ALU.subtract).then_inc(o_lo, 1)

            l0, l1 = par[:, prow["lb0"]:prow["lb0"] + 4], par[:, prow["lb1"]:prow["lb1"] + 4]
            ch.link(dve.tensor_tensor(cm[:, 0:4], l0, l1, ALU.max))
            dve.tensor_tensor(cm[:, 4:8], l0, cm[:, 0:4], ALU.subtract).then_inc(s_lb, 1)
            dve.tensor_tensor(cm[:, 8:12], l1, cm[:, 0:4], ALU.subtract).then_inc(s_lb, 1)
            dve.wait_ge(s_lb, 3)
            ch.link(dve.tensor_tensor(cm[:, 12:16], cm[:, 4:8], cm[:, 8:12], ALU.add))
            ch.link(dve.reciprocal(cm[:, 16:20], cm[:, 12:16]))
            ch.link(dve.tensor_tensor(lb, cm[:, 4:8], cm[:, 16:20], ALU.mult))
            ch.link(dve.tensor_scalar(oml, lb, -1.0, 1.0, ALU.mult, ALU.add))
            dve.wait_ge(chunk_done, 4)
            ch.link(dve.memset(att, 0.0))
            key_gates(0)
            decays(0)
            keys(0)
            queries(0)
            dve.wait_ge(s_m0in, 64)
            for u in range(NU):
                if u > 0:
                    head_gate(u - 1, last(u - 1))
                mask_scores(u, 0)
                if last(u):
                    mask_scores(u, 1)
                if u > 0:
                    head_lo(u - 1, last(u - 1))
                    dve.wait_ge(m0_out, 32 * heads_before[u])
                if u + 1 < NU:
                    key_gates(u + 1)
                states(u)
                if u + 1 < NU:
                    decays(u + 1)
                    keys(u + 1)
                final_states(u)
                if u + 1 < NU:
                    queries(u + 1)
                for step in (head_norm, out_gate) if u + 1 < NU else (out_gate, head_norm):
                    step(u, 0)
                if last(u):
                    head_gate(u, 0)
                    head_lo(u, 0)
                    head_norm(u, 1)
                    out_gate(u, 1)
            head_gate(NU - 1, last(NU - 1))
            head_lo(NU - 1, last(NU - 1))
            add_back(1, C_O0)
            ffn(0)
            def logf_and_cum():
                dve.wait_ge(tb_out, NT)
                wait_freed(dve, C_M1)
                dve.wait_ge(s_m1in, 16 * 8)
                for m, i0, i1 in token_tiles:
                    bias = fb[0:m].rearrange("p (o n) -> p o n", o=1).broadcast_to([m, i1 - i0, CH])
                    dve.tensor_tensor(lf_z[0:m, i0:i1], stage[0:m, i0:i1, OFG - P:TBW - P], bias, ALU.add).then_inc(lf_biased, 1)
                for n, (m, i0, i1) in enumerate(token_tiles):
                    dve.wait_ge(lf_abs, n + 1)
                    dve.scalar_tensor_tensor(out=lft[0:m, i0:i1], in0=lf_z[0:m, i0:i1], scalar=0.0, in1=lf_a[0:m, i0:i1],
                                             op0=ALU.min, op1=ALU.subtract).then_inc(lf_ready, 1)
                dve.wait_ge(lf_out, 3)
                for n0, n1 in ((0, TP), (TP, W)):
                    ch.link(dve.tensor_tensor_scan(lf_cum[:, n0:n1], ones[0:CH, 0:1].broadcast_to([CH, n1 - n0]), lf[:, n0:n1], 0.0,
                                                   ALU.mult, ALU.add))
                ch.link(dve.tensor_scalar(lf_cum, lf_cum, -8.0, None, ALU.mult))
                dve.wait_ge(s_m1c, 3)
                for b in range(3):
                    part = cp[32 * b:32 * b + CH, :]
                    ins = dve.tensor_copy(part, lf_cum)
                    if b < 2:
                        ch.link(ins)
                        ch.link(dve.tensor_tensor(lf_cum, lf_cum, part, ALU.subtract))
                    else:
                        ins.then_inc(cp_done, 1)

            def add_scores(n):
                m = P if n < 3 else TS
                i = n + 1
                for h in range(4):
                    w_ = stage[0:m, i, 5 * IDX + h:5 * IDX + h + 1]
                    dve.wait_ge(sc_relu, 4 * n + h + 1)
                    r = relu[0:m, h, 0:nks[n]]
                    if h == 0:
                        dve.tensor_scalar(idx[n][0:m, :], r, w_, None, ALU.mult).then_inc(sc_acc, 1)
                    else:
                        dve.wait_ge(sc_acc, 4 * n + h)
                        dve.scalar_tensor_tensor(out=idx[n][0:m, :], in0=r, scalar=w_, in1=idx[n][0:m, :], op0=ALU.mult, op1=ALU.add)\
                           .then_inc(sc_acc, 1)

            def mask_later(n):
                ch.link(dve.memset(idx[n][0:CHUNK, nks[n] - CHUNK:nks[n]], NEG))

            def largest(n):
                m = P if n < 3 else TS
                if n in pending:
                    dve.wait_ge(dve_s, pending[n])
                pending[n] = ch.add(dve.max(m8[n][0:m, :], idx[n][0:m, :]))

            def replace(n):
                m = P if n < 3 else TS
                dve.wait_ge(dve_s, pending[n])
                pending[n] = ch.add(dve.match_replace(idx[n][0:m, :], m8[n][0:m, :], idx[n][0:m, :], TAKEN))

            def chosen(n):
                m = P if n < 3 else TS
                dve.wait_ge(dve_s, pending[n])
                ch.link(dve.tensor_scalar(mb[n + 1][0:m, :], idx[n][0:m, :], TAKEN / 2, NEG, ALU.is_gt, ALU.mult))

            def attention(dsa):
                X0, PX = NX * dsa, 5 * dsa

                def maxima(x):
                    dve.wait_ge(at_l, X0 + x + 1)
                    tl = groups[x][1] or [(NT, 0, KS)]
                    for j, (i, c, nk) in enumerate(tl):
                        ch.add(dve.tensor_reduce(mx[:, x % 4, j:j + 1], ps[:, x % 4, c:c + nk], AX_X, ALU.max))
                    dve.wait_ge(dve_s, ch.n)
                    dve.tensor_scalar(nmx[:, x % 4, 0:len(tl)], mx[:, x % 4, 0:len(tl)], -1.0 / 8.0, None, ALU.mult).then_inc(at_mx, 1)

                def normalise(x):
                    dve.wait_ge(at_e, X0 + x + 1)
                    tl = groups[x][1] or [(NT, 0, KS)]
                    ch.link(dve.reciprocal(rec[:, x % 4, 0:len(tl)], psums[:, x % 4, 0:len(tl)]))
                    for j, (i, c, nk) in enumerate(tl):
                        p_ = prob[:, x % 3, c:c + nk]
                        ins = dve.tensor_scalar(p_, p_, rec[:, x % 4, j:j + 1], None, ALU.mult)
                    ins.then_inc(at_p, 1)

                def outputs(x):
                    pi = pairs_end.index(x)
                    dve.wait_ge(at_h, PX + pi + 1)
                    b = ps[:, 6 + (PX + pi) % 2, :]
                    if pi < 4:
                        o, hh = ol[:, 4 * dsa + pi, 0:TP], oh[:, 4 * dsa + pi, 0:TP]
                    else:
                        o, hh = ol[:, 4 * dsa:4 * dsa + 4, TP:T], oh[:, 4 * dsa:4 * dsa + 4, TP:T]
                        b = b[:, 0:4 * TS].rearrange("p (t n) -> p t n", t=4)
                    dve.tensor_tensor(o, b, hh.bitcast(F32), ALU.subtract).then_inc(at_o, 1)

                maxima(0)
                maxima(1)
                normalise(0)
                for x in range(NX + 3):
                    late = 3 if not dsa and 1 <= x <= LATE else None
                    if late is not None:
                        largest(late)
                    if x + 2 < NX:
                        maxima(x + 2)
                    if x + 1 < NX:
                        normalise(x + 1)
                    if x - 3 in pairs_end:
                        outputs(x - 3)
                    if late is not None:
                        replace(late)
                        if x == LATE:
                            chosen(late)

            LATE = 5
            pending = {}

            def rounds(tiles, n):
                for r in range(n):
                    for step in (largest, replace):
                        for tile in tiles:
                            step(tile)

            logf_and_cum()
            QUARTER = TOPP // 32
            for n in range(4):
                add_scores(n)
                if n < 3:
                    dve.wait_ge(sc_acc, 4 * (n + 1))
                    mask_later(n)
                    rounds([0, 1][:n + 1], QUARTER)
            dve.wait_ge(sc_acc, 16)
            rounds([0, 2], QUARTER)
            chosen(0)
            rounds([1, 2], 2 * QUARTER)
            chosen(1)
            rounds([2, 3], QUARTER)
            chosen(2)
            rounds([3], TOPS // 8 - QUARTER - LATE)
            attention(0)
            for c in [C_DK] + C_DQ:
                dst = kT[:, 0, :] if c == C_DK else qT[:, c - C_DQ[0], :]
                wait_done(dve, c)
                dve.tensor_tensor(two(dst), pair(c), two(rstd[:, :]), ALU.mult).then_inc(frees(c), 1)
            attention(1)
            add_back(3, C_O1)
            ffn(1)
            dve.wait_ge(s_rt, 2)
            for m, i0, i1 in token_tiles:
                ch.add(dve.reciprocal(rcol[0:m, i0:i1], rcol[0:m, i0:i1]))
            dve.wait_ge(dve_s, ch.n)
            for i in range(NT + 1):
                n = P if i < NT else TS
                dve.wait_ge(y_turned, i + 1)
                dve.tensor_scalar(y_sb[0:n, i, :].rearrange("p (b t) -> p b t", b=2), ps[0:n, 2 * (i % 2):2 * (i % 2) + 2, :],
                                  rcol[0:n, i:i + 1], None, ALU.mult).then_inc(y_ready, 1)
    return nc


_INS = ["x_prompt", "x_sample", "state_hgrn", "state_gla", "cache_fox_k", "cache_fox_v", "cache_fox_logf",
        "cache_dsa_k", "cache_dsa_v", "cache_dsa_ik", "norm_mix", "norm_ffn", "norm_final", "ab_w_in", "ab_w_out",
        "hgrn_lb_logits", "hgrn_gnorm", "gla_w_gk", "gla_b_gk", "gla_gnorm", "cd_w_in", "cd_w_out", "fox_f_bias",
        "ffn_w_in", "ffn_w_out"]
_OUTS = ["y_prompt", "y_sample", "p_hgrn", "p_gla", "p_fox_k", "p_fox_v", "p_fox_logf", "p_dsa_k", "p_dsa_v",
         "p_dsa_ik", "s_hgrn", "s_gla", "s_fox_k", "s_fox_v", "s_fox_logf", "s_dsa_k", "s_dsa_v", "s_dsa_ik"]


def kernel(**inputs):
    import numpy as np
    import concourse.bacc as bacc
    from concourse.bass_utils import run_bass_kernel_spmd as run

    nc = bacc.Bacc("TRN2", target_bir_lowering=False, num_devices=1)
    arrays, I, O = {}, {}, {}
    for name in _INS:
        a = np.ascontiguousarray(inputs[name])
        arrays[f"in_{name}"] = a
        I[name] = nc.dram_tensor(f"in_{name}", a.shape, mybir.dt.from_np(a.dtype), kind="ExternalInput").ap()
    xp, xs = inputs["x_prompt"].shape, inputs["x_sample"].shape
    shapes = {"y_prompt": xp, "y_sample": xs, "p_hgrn": inputs["state_hgrn"].shape, "p_gla": inputs["state_gla"].shape,
              "s_hgrn": inputs["state_hgrn"].shape, "s_gla": inputs["state_gla"].shape}
    for q, t in (("p", xp[1]), ("s", xs[1])):
        for n in ("fox_k", "fox_v", "fox_logf", "dsa_k", "dsa_v", "dsa_ik"):
            c = inputs["cache_" + n].shape
            shapes[f"{q}_{n}"] = (*c[:2], t, *c[3:])
    for name in _OUTS:
        O[name] = nc.dram_tensor(f"out_{name}", tuple(shapes[name]), F32, kind="ExternalOutput").ap()
    build(nc, I, O)
    r = run(nc, [arrays], core_ids=[0])
    return tuple(r.results[0][f"out_{name}"] for name in _OUTS)
```
